# Optimizing a Trainium2 kernel written in Bass

```python
import math
import jax, jax.numpy as jnp
from jax import lax
import numpy as np

D_MODEL = 1024
BATCH = 1
SEQ = 256
DEPTH = 2

D_MIX = D_MODEL
D_ATTN = D_MIX // 2
D_CONV = D_MIX - D_ATTN
N_HEADS = 4
QK_NOPE = 128
QK_ROPE = 64
V_HEAD = D_ATTN // N_HEADS
Q_LORA = 256
KV_LORA = 128
CONV_WIDTH = 3
D_IN = Q_LORA + KV_LORA + QK_ROPE + 3 * D_CONV
ROPE_BASE = 10000.0
Q_BLOCK = 128
D_FF = 2816
N_EXPERTS = 8
TOP_K = 2
D_FF_EXPERT = 3584
N_DENSE = (DEPTH + 1) // 2
N_MOE = DEPTH // 2
RMS_EPS = 1e-6
LN_EPS = 1e-5
DEEPNORM_ALPHA = (2 * DEPTH) ** 0.25
DEEPNORM_BETA = (8 * DEPTH) ** -0.25
ADA_INIT_SCALE = 0.1

kernel_name = "hybrid_mla_shortconv_moe_deepnorm_adaln"

def rms_norm(x, g):
    xf = x.astype(jnp.float32)
    y = xf * lax.rsqrt(jnp.mean(xf * xf, axis=-1, keepdims=True) + RMS_EPS)
    return (y * g.astype(jnp.float32)).astype(x.dtype)

def layer_norm(x, g, b):
    xf = x.astype(jnp.float32)
    mu = jnp.mean(xf, axis=-1, keepdims=True)
    var = jnp.mean(jnp.square(xf - mu), axis=-1, keepdims=True)
    y = (xf - mu) * lax.rsqrt(var + LN_EPS) * g.astype(jnp.float32) + b.astype(jnp.float32)
    return y.astype(x.dtype)

def rope_angles(positions):
    inv_freq = ROPE_BASE ** (-jnp.arange(0, QK_ROPE, 2, dtype=jnp.float32) / QK_ROPE)
    ang = positions.astype(jnp.float32)[..., None] * inv_freq
    return jnp.cos(ang), jnp.sin(ang)

def apply_rope(x, cos, sin):
    half = x.shape[-1] // 2
    x1 = x[..., :half].astype(jnp.float32)
    x2 = x[..., half:].astype(jnp.float32)
    y = jnp.concatenate([x1 * cos - x2 * sin, x2 * cos + x1 * sin], axis=-1)
    return y.astype(x.dtype)

def causal_mla_attention(q_nope, q_rope, k_nope, k_rope, v):
    b, s, h, _ = q_nope.shape
    nb = s // Q_BLOCK
    scale = (QK_NOPE + QK_ROPE) ** -0.5
    qn = q_nope.reshape(b, nb, Q_BLOCK, h, QK_NOPE).transpose(1, 0, 2, 3, 4)
    qr = q_rope.reshape(b, nb, Q_BLOCK, h, QK_ROPE).transpose(1, 0, 2, 3, 4)
    key_pos = jnp.arange(s)

    def one_block(args):
        qn_b, qr_b, i = args
        sc = (jnp.einsum('bqhd,bkhd->bhqk', qn_b, k_nope)
              + jnp.einsum('bqhr,bkr->bhqk', qr_b, k_rope)).astype(jnp.float32) * scale
        q_pos = i * Q_BLOCK + jnp.arange(Q_BLOCK)
        mask = key_pos[None, :] <= q_pos[:, None]
        sc = jnp.where(mask[None, None], sc, jnp.finfo(jnp.float32).min)
        p = jax.nn.softmax(sc, axis=-1).astype(v.dtype)
        return jnp.einsum('bhqk,bkhd->bqhd', p, v)

    out = lax.map(one_block, (qn, qr, jnp.arange(nb)))
    return out.transpose(1, 0, 2, 3, 4).reshape(b, s, h * V_HEAD)

def causal_short_conv(u, w):
    s = u.shape[1]
    up = jnp.pad(u, ((0, 0), (CONV_WIDTH - 1, 0), (0, 0)))
    return sum(w[j] * up[:, j:j + s] for j in range(CONV_WIDTH))

def hybrid_mixer(h, cos, sin, w_in, q_norm_g, kv_norm_g, w_uq, w_ukv, conv_w, mix_norm_g, w_o):
    b, s, _ = h.shape
    z = h @ w_in
    o1 = Q_LORA
    o2 = o1 + KV_LORA
    o3 = o2 + QK_ROPE
    o4 = o3 + D_CONV
    o5 = o4 + D_CONV
    c_q, c_kv, k_rope = z[..., :o1], z[..., o1:o2], z[..., o2:o3]
    gate_b, gate_c, u = z[..., o3:o4], z[..., o4:o5], z[..., o5:]
    q = (rms_norm(c_q, q_norm_g) @ w_uq).reshape(b, s, N_HEADS, QK_NOPE + QK_ROPE)
    kv = (rms_norm(c_kv, kv_norm_g) @ w_ukv).reshape(b, s, N_HEADS, QK_NOPE + V_HEAD)
    q_nope, q_rope = q[..., :QK_NOPE], q[..., QK_NOPE:]
    k_nope, v = kv[..., :QK_NOPE], kv[..., QK_NOPE:]
    q_rope = apply_rope(q_rope, cos[:, :, None, :], sin[:, :, None, :])
    k_rope = apply_rope(k_rope, cos, sin)
    attn = causal_mla_attention(q_nope, q_rope, k_nope, k_rope, v)
    conv = gate_b * causal_short_conv(gate_c * u, conv_w)
    y = jnp.concatenate([rms_norm(attn, mix_norm_g[:D_ATTN]),
                         rms_norm(conv, mix_norm_g[D_ATTN:])], axis=-1)
    return y @ w_o

def swiglu(h, wg, wu, wd):
    return (jax.nn.silu(h @ wg) * (h @ wu)) @ wd

def top2_moe(h, router_w, router_b, wg, wu, wd):
    b, s, d = h.shape
    t = h.reshape(b * s, d)
    logits = (t @ router_w).astype(jnp.float32) + router_b.astype(jnp.float32)
    top_v, top_i = lax.top_k(logits, TOP_K)
    gates = jax.nn.softmax(top_v, axis=-1)
    combine = jnp.sum(jax.nn.one_hot(top_i, N_EXPERTS, dtype=jnp.float32) * gates[..., None], axis=1)
    combine = combine.astype(h.dtype)
    out = jnp.zeros_like(t)
    for e in range(N_EXPERTS):
        out = out + combine[:, e:e + 1] * swiglu(t, wg[e], wu[e], wd[e])
    return out.reshape(b, s, d)

def setup_inputs(seed: int = 0) -> dict:
    key = jax.random.key(seed)
    ks = iter(jax.random.split(key, 32))
    nrm = lambda shape, std: jax.random.normal(next(ks), shape, jnp.float32) * std
    gain = lambda shape: 1.0 + nrm(shape, 0.01)
    L = DEPTH
    x = nrm((BATCH, SEQ, D_MODEL), 1.0)
    c = nrm((BATCH, D_MODEL), 1.0)
    positions = (jnp.arange(SEQ, dtype=jnp.int32)[None, :]
                 + jax.random.randint(next(ks), (BATCH, 1), 0, 1024, dtype=jnp.int32))
    b_ada = nrm((L, 6, D_MODEL), 0.01)
    b_ada = b_ada.at[:, 2].add(1.0).at[:, 5].add(1.0).reshape(L, 6 * D_MODEL)
    return {
        "x": x,
        "c": c,
        "positions": positions,
        "w_in": nrm((L, D_MODEL, D_IN), D_MODEL ** -0.5),
        "q_norm_g": gain((L, Q_LORA)),
        "kv_norm_g": gain((L, KV_LORA)),
        "w_uq": nrm((L, Q_LORA, N_HEADS * (QK_NOPE + QK_ROPE)), Q_LORA ** -0.5),
        "w_ukv": nrm((L, KV_LORA, N_HEADS * (QK_NOPE + V_HEAD)), KV_LORA ** -0.5),
        "conv_w": nrm((L, CONV_WIDTH, D_CONV), CONV_WIDTH ** -0.5),
        "mix_norm_g": gain((L, D_MIX)),
        "w_o": nrm((L, D_MIX, D_MODEL), D_MIX ** -0.5 * DEEPNORM_BETA),
        "w_ada": nrm((L, D_MODEL, 6 * D_MODEL), D_MODEL ** -0.5 * ADA_INIT_SCALE),
        "b_ada": b_ada,
        "ln1_g": gain((L, D_MODEL)),
        "ln1_b": nrm((L, D_MODEL), 0.01),
        "ln2_g": gain((L, D_MODEL)),
        "ln2_b": nrm((L, D_MODEL), 0.01),
        "ffn_w_gate": nrm((N_DENSE, D_MODEL, D_FF), D_MODEL ** -0.5),
        "ffn_w_up": nrm((N_DENSE, D_MODEL, D_FF), D_MODEL ** -0.5),
        "ffn_w_down": nrm((N_DENSE, D_FF, D_MODEL), D_FF ** -0.5 * DEEPNORM_BETA),
        "moe_router_w": nrm((N_MOE, D_MODEL, N_EXPERTS), D_MODEL ** -0.5),
        "moe_router_b": nrm((N_MOE, N_EXPERTS), 0.01),
        "moe_w_gate": nrm((N_MOE, N_EXPERTS, D_MODEL, D_FF_EXPERT), D_MODEL ** -0.5),
        "moe_w_up": nrm((N_MOE, N_EXPERTS, D_MODEL, D_FF_EXPERT), D_MODEL ** -0.5),
        "moe_w_down": nrm((N_MOE, N_EXPERTS, D_FF_EXPERT, D_MODEL), D_FF_EXPERT ** -0.5 * DEEPNORM_BETA),
    }

def reference(x, c, positions, w_in, q_norm_g, kv_norm_g, w_uq, w_ukv, conv_w, mix_norm_g, w_o,
              w_ada, b_ada, ln1_g, ln1_b, ln2_g, ln2_b, ffn_w_gate, ffn_w_up, ffn_w_down,
              moe_router_w, moe_router_b, moe_w_gate, moe_w_up, moe_w_down):
    cos, sin = rope_angles(positions)
    c_act = jax.nn.silu(c)
    for l in range(DEPTH):
        mod = (c_act @ w_ada[l] + b_ada[l])[:, None, :]
        shift1, scale1, gate1, shift2, scale2, gate2 = jnp.split(mod, 6, axis=-1)
        h = x * (1 + scale1) + shift1
        y = hybrid_mixer(h, cos, sin, w_in[l], q_norm_g[l], kv_norm_g[l], w_uq[l], w_ukv[l],
                         conv_w[l], mix_norm_g[l], w_o[l])
        x = layer_norm(DEEPNORM_ALPHA * x + gate1 * y, ln1_g[l], ln1_b[l])
        h = x * (1 + scale2) + shift2
        if l % 2 == 0:
            i = l // 2
            f = swiglu(h, ffn_w_gate[i], ffn_w_up[i], ffn_w_down[i])
        else:
            i = l // 2
            f = top2_moe(h, moe_router_w[i], moe_router_b[i], moe_w_gate[i], moe_w_up[i], moe_w_down[i])
        x = layer_norm(DEEPNORM_ALPHA * x + gate2 * f, ln2_g[l], ln2_b[l])
    return x


_drawn_inputs = setup_inputs


def setup_inputs(seed=0):
    import zlib

    import numpy as np

    out = dict(_drawn_inputs(seed))
    spreads = {}
    factors = {'q_norm_g': 6.894,
     'kv_norm_g': 8.0,
     'mix_norm_g': 8.0,
     'ln1_g': 2.713,
     'ln2_g': 3.415,
     'moe_router_b': 31.567,
     'ln2_b': 2.863}
    for name, (base, spread) in spreads.items():
        noise = np.random.default_rng([zlib.crc32(name.encode()), seed]).standard_normal(out[name].shape)
        drawn = base * np.exp(spread * noise) if base else spread * noise
        out[name] = __import__('jax').numpy.asarray(drawn.astype(out[name].dtype))
    for name, factor in factors.items():
        out[name] = (out[name] * factor).astype(out[name].dtype)
    return out
```

```python
from contextlib import ExitStack

import numpy as np

import concourse.bass as bass
from concourse import mybir

F32 = mybir.dt.float32
F32R = mybir.dt.float32r
I32 = mybir.dt.int32
ALU = mybir.AluOpType
ACT = mybir.ActivationFunctionType
AX_X = mybir.AxisListType.X

P = 128
D = 1024
KC = D // P
T = 256
TT = T // P
L = 2
HEADS, NOPE, ROPE, VH = 4, 128, 64, 128
HALF = ROPE // 2
Q_LORA, KV_LORA = 256, 128
ZA = Q_LORA + KV_LORA + ROPE
D_CONV = 512
CC = D_CONV // P
FF = 2816
FF_STEPS = FF // 256
E = 8
FE = 3584
E_STEPS = FE // 512
OVER = 3
ITEMS = E + OVER
SCALE = float(NOPE + ROPE) ** -0.5
ALPHA = float((2 * L) ** 0.25)
RMS_EPS, LN_EPS = 1e-6, 1e-5
MASKED = -1e30
ROPE_BASE = 10000.0
TWO_PI = 2.0 * np.pi

RING = 7
SLOT = 4096
UNIT = 1024
SRING = 4
HEAD = 3
SCATTER_BANKS = ((5, 6), (7, 2))
GATE_BANKS = (0, 7)
FF_UNITS = 6 * FF_STEPS
E_UNITS = 12 * E_STEPS
E_LOADS = 3 * E_STEPS

PRM_L = Q_LORA // P + KV_LORA // P + KC + 3 * CC
PRM = KC + L * PRM_L
STRIPS = 6 * D // 512

BANK7 = ["params"] + [("ada", 0, n) for n in range(4)]
BANK7 += [("ada", 0, n) for n in range(4, 9)] + [("ssq_conv", 0), ("ada", 0, 9), ("ssq_attn", 0)]
BANK7 += [("ada", 0, 10), ("ada", 0, 11)] + [("ada", 1, n) for n in range(10)]
BANK7 += [("ssq_conv", 1), ("ada", 1, 10), ("ada", 1, 11), ("ssq_attn", 1)]
ADA_ORDER = [u for u in BANK7 if u[0] == "ada"]

FF_ADA = {s: [("ada", 1, s - 1)] for s in range(1, FF_STEPS)}
FF_ADA[0] = [("ada", 0, 10), ("ada", 0, 11)]


def split2pi():
    parts, rest = [], TWO_PI
    for bits in (8, 9, 9):
        scale = 2.0 ** (bits - 1 - np.floor(np.log2(abs(rest))))
        part = float(np.floor(rest * scale) / scale)
        parts.append(part)
        rest -= part
    parts.append(float(np.float32(rest)))
    return parts


def ff_first_unit(s):
    return 0 if s == 0 else 4 + 6 * (s - 1)


def moe_first_unit(j):
    return 0 if j == 0 else 8 + 12 * (j - 1)


def trunk(nc, a, out):
    with ExitStack() as ctx:
        def sb(name, shape, dt=F32, stack=ctx):
            return stack.enter_context(nc.sbuf_tensor(name, shape, dt))

        sems = {}

        def sem(name):
            sems[name] = ctx.enter_context(nc.semaphore(name))
            return sems[name]

        ps = ctx.enter_context(nc.psum_tensor("ps", [P, 8, 512], F32))

        raw = sb("raw", [P, RING, SLOT])
        x_sb = sb("x_sb", [P, TT, D])
        yv = sb("yv", [P, TT, D])
        h_t = sb("h_t", [P, KC, T])
        ln_g = sb("ln_g", [P, D])
        ln_b = sb("ln_b", [P, D])
        gate1 = sb("gate1", [P, D])
        gate2 = sb("gate2", [P, D])
        ada_acc = sb("ada_acc", [P, 2, 512])
        ada_bias = sb("ada_bias", [STRIPS, L, 512])
        ident = sb("ident", [P, P])
        ones = sb("ones", [P, P])
        causal = sb("causal", [P, P])
        before = sb("before", [P, P])
        slot_no = sb("slot_no", [P, P])
        slot_i = sb("slot_i", [P, P], I32)
        prm_rows = sb("prm_rows", [PRM, P])
        prm = sb("prm", [P, PRM])
        c_act = sb("c_act", [P, KC])
        modc = sb("modc", [P, L, 4, KC])
        pos_i = sb("pos_i", [P, TT], I32)
        pos_f = sb("pos_f", [P, TT])
        freq = sb("freq", [P, HALF])
        trig = sb("trig", [P, 2, TT, HALF])
        ang = sb("ang", [P, 2, TT, HALF])
        turns = sb("turns", [P, 2, TT, HALF])
        eps = sb("eps", [P, 3])
        stats = sb("stats", [P, TT, 2, 6])
        meanvar = sb("meanvar", [P, TT, 2])
        std = sb("std", [P, TT])
        rstd = sb("rstd", [P, TT])
        ssq = sb("ssq", [P, 2, TT])
        rms = sb("rms", [P, 2, TT])
        rrms = sb("rrms", [P, 2, TT])
        gstd = sb("gstd", [P, 2, TT])
        grr = sb("grr", [P, 2, TT])
        mx = sb("mx", [P, TT, HEADS])
        nmx = sb("nmx", [P, TT, HEADS])
        den = sb("den", [P, TT, HEADS])
        rden = sb("rden", [P, TT, HEADS])
        router_w = sb("router_w", [P, KC, E])
        router_b = sb("router_b", [1, E])
        logit = sb("logit", [P, TT, E])
        top = sb("top", [P, TT, 8])
        above = sb("above", [P, TT, E])
        pads = sb("pads", [P, 3, TT, 2 * E])
        n_above = sb("n_above", [P, TT])
        chosen = sb("chosen", [P, TT, E])
        expo = sb("expo", [P, TT, E])
        exsum = sb("exsum", [P, TT])
        exinv = sb("exinv", [P, TT])
        place = sb("place", [P, TT, ITEMS + 1])
        share = sb("share", [P, TT, ITEMS + 1])
        cnt = sb("cnt", [P, 3, 2 * E])
        rank = sb("rank", [P, E])
        e_no = sb("e_no", [P, E])
        pick = sb("pick", [P, OVER, E])
        picked = sb("picked", [P, OVER, 5, E])
        plan_f = sb("plan_f", [P, 1 + OVER])
        plan_i = sb("plan_i", [P, 1 + OVER], I32)

        mix = ExitStack()
        zn = sb("zn", [P, TT, Q_LORA + KV_LORA], stack=mix)
        kr = sb("kr", [P, TT, 2, 2, ROPE], stack=mix)
        cq_t = sb("cq_t", [P, 2, T], stack=mix)
        ckv_t = sb("ckv_t", [P, T], stack=mix)
        kr_t = sb("kr_t", [P, 2, T], stack=mix)
        qr = sb("qr", [P, TT, HEADS, ROPE], stack=mix)
        qr_t = sb("qr_t", [P, 2, T], stack=mix)
        qn_t = sb("qn_t", [P, HEADS, T], stack=mix)
        kn_t = sb("kn_t", [P, HEADS, T], stack=mix)
        v_sb = sb("v_sb", [P, TT, HEADS * VH], stack=mix)
        gb_t = sb("gb_t", [P, CC, T], stack=mix)
        gc_t = sb("gc_t", [P, CC, T], stack=mix)
        cu = sb("cu", [P, CC, T + 2], stack=mix)
        cv = sb("cv", [P, CC, T], stack=mix)
        mix.close()
        rp_k = cv[:, 0, :].rearrange("p (k t r) -> p k t r", k=4, t=TT)
        rp_q = cv[:, :, :].rearrange("p k (t h r) -> p k t h r", t=TT, h=HEADS)
        p0 = zn[:, :, :].rearrange("p t n -> p (t n)")[:, 0:HEADS * P].rearrange("p (h s) -> p h s", h=HEADS)
        p1, cv_t, a_t = gb_t, gc_t, cv
        p_t0, p_t1 = qn_t, kn_t[:, :, 0:P]
        sq = h_t[:, 0:CC, :]
        ff = ExitStack()
        w_hi = sb("w_hi", [P, SRING, UNIT], F32R, ff)
        w_lo = sb("w_lo", [P, SRING, UNIT], F32R, ff)
        h_hi = sb("h_hi", [P, KC, T], F32R, ff)
        h_lo = sb("h_lo", [P, KC, T], F32R, ff)
        sil = sb("sil", [P, 512], stack=ff)
        hid_hi = sb("hid_hi", [P, 512], F32R, ff)
        hid_lo = sb("hid_lo", [P, 512], F32R, ff)
        hid = h_t[:, 4:8, P:T]
        sel = h_t[:, 0:2, P:T]
        sel_t = h_t[:, 2:4, P:T]
        y_sb = ada_acc[:, :, :].rearrange("p b n -> p (b n)")
        ff.close()
        moe_acc = yv
        xg_hi, xg_lo, xg = h_hi[:, :, 0:P], h_lo[:, :, 0:P], h_t[:, :, 0:P]

        slot_full = [sem(f"slot_full{k}") for k in range(RING)]
        ada_summed = sem("ada_summed")
        unit_hi, unit_lo, unit_used = sem("unit_hi"), sem("unit_lo"), sem("unit_used")
        prm_loaded, x_loaded, ln_loaded, rt_loaded = (sem("prm_loaded"), sem("x_loaded"), sem("ln_loaded"),
                                                      sem("rt_loaded"))
        const_order, consts = sem("const_order"), sem("consts")
        dve_order, act_order = sem("dve_order"), sem("act_order")
        bank7_full, bank7_free = sem("bank7_full"), sem("bank7_free")
        c_ready, angles, trig_ready = sem("c_ready"), sem("angles"), sem("trig_ready")
        x_ready, xt_mm, ht_ready = sem("x_ready"), sem("xt_mm"), sem("ht_ready")
        h_hi_ready, h_lo_ready = sem("h_hi_ready"), sem("h_lo_ready")
        za_mm, zb_mm, zc_mm, zu_mm = sem("za_mm"), sem("zb_mm"), sem("zc_mm"), sem("zu_mm")
        gb_ready, gc_ready, cu_ready = sem("gb_ready"), sem("gc_ready"), sem("cu_ready")
        ssq_ready, rms_ready, zn_ready = sem("ssq_ready"), sem("rms_ready"), sem("zn_ready")
        znt_mm, znt_ready = sem("znt_mm"), sem("znt_ready")
        qn_mm, kn_mm, qr_mm, v_mm = sem("qn_mm"), sem("kn_mm"), sem("qr_mm"), sem("v_mm")
        qn_ready, kn_ready, qr_ready, v_ready = (sem("qn_ready"), sem("kn_ready"), sem("qr_ready"),
                                                 sem("v_ready"))
        qrt_mm, qrt_ready = sem("qrt_mm"), sem("qrt_ready")
        score_mm, max_ready, exp_ready, prob_ready = (sem("score_mm"), sem("max_ready"), sem("exp_ready"),
                                                      sem("prob_ready"))
        pt_mm, pt_ready = sem("pt_mm"), sem("pt_ready")
        conv_ready, conv_sq, conv_scaled = sem("conv_ready"), sem("conv_sq"), sem("conv_scaled")
        gstd_ready, grr_ready = sem("gstd_ready"), sem("grr_ready")
        yc_mm, yc_ready = sem("yc_mm"), sem("yc_ready")
        attn_mm, attn_sq, attn_scaled, ya_mm = sem("attn_mm"), sem("attn_sq"), sem("attn_scaled"), sem("ya_mm")
        var_ready, std_ready = sem("var_ready"), sem("std_ready")
        silu_done, hid_done = sem("silu_done"), sem("hid_done")
        hidt_mm, hidt_hi, hidt_lo = sem("hidt_mm"), sem("hidt_hi"), sem("hidt_lo")
        logit_mm, rel_ready, expo_ready, chosen_ready = (sem("logit_mm"), sem("rel_ready"), sem("expo_ready"),
                                                         sem("chosen_ready"))
        place_mm, plan_ready = sem("place_mm"), sem("plan_ready")
        sel_ready, selt_mm, selt_ready = sem("sel_ready"), sem("selt_mm"), sem("selt_ready")
        xg_mm, xg_ready, xg_hi_ready, xg_lo_ready = (sem("xg_mm"), sem("xg_ready"), sem("xg_hi_ready"),
                                                     sem("xg_lo_ready"))
        y_ready, y2_ready, scatter_mm, acc_ready = (sem("y_ready"), sem("y2_ready"), sem("scatter_mm"),
                                                    sem("acc_ready"))
        xg2_ready, xg2_hi = sem("xg2_ready"), sem("xg2_hi")
        out_done = sem("out_done")

        def strip_src(l, n):
            return a["w_ada"][l][:, n * 512:(n + 1) * 512].rearrange("(c p) n -> p c n", p=P)

        def win_src(l, lo, hi):
            return a["w_in"][l][:, lo:hi].rearrange("(c p) n -> p c n", p=P)

        loads = []

        def load_ada(l, n):
            k = ADA_ORDER.index(("ada", l, n))
            loads.append((("ada", l, n), [(0, 4096, KC, strip_src(l, n))], (ada_summed, k + 1)))

        def load_pe(name, parts, released):
            loads.append((name, parts, released))

        for n in range(4):
            load_ada(0, n)
        for l in range(L):
            z0 = ZA
            load_pe(("wa", l), [(0, KC * ZA, KC, win_src(l, 0, ZA))], (za_mm, TT * (l + 1)))
            load_pe(("wb", l), [(0, SLOT, KC, win_src(l, z0, z0 + D_CONV))], (zb_mm, l + 1))
            load_pe(("wc", l), [(0, SLOT, KC, win_src(l, z0 + D_CONV, z0 + 2 * D_CONV))], (zc_mm, l + 1))
            if l == 0:
                for n in (4, 5, 6):
                    load_ada(0, n)
            load_pe(("wu", l), [(0, SLOT, KC, win_src(l, z0 + 2 * D_CONV, z0 + 3 * D_CONV))], (zu_mm, l + 1))
            if l == 0:
                for n in (7, 8):
                    load_ada(0, n)
            load_pe(("qkv", l), [(0, 2 * 768, 2, a["w_uq"][l].rearrange("(c p) n -> p c n", p=P)),
                                 (2 * 768, 2 * 768 + 1024, 1, a["w_ukv"][l].rearrange("(c p) n -> p c n", p=P))], (v_mm, l + 1))
            for n in ((9,), (10, 11))[l]:
                load_ada(l, n)
            load_pe(("oc", l), [(0, SLOT, 4, a["w_o"][l][512:1024, :].rearrange("(c p) n -> p c n", p=P))],
                    (yc_mm, TT * (l + 1)))
            load_pe(("oa", l), [(0, SLOT, 4, a["w_o"][l][0:512, :].rearrange("(c p) n -> p c n", p=P))],
                    (ya_mm, TT * (l + 1)))
            if l == 0:
                for s in range(FF_STEPS + 1):
                    if s < FF_STEPS:
                        cols = slice(s * 256, (s + 1) * 256)
                        loads.append((("gu", s), [
                            (0, 2048, KC, a["ffn_w_gate"][0][:, cols].rearrange("(c p) n -> p c n", p=P)),
                            (2048, 4096, KC, a["ffn_w_up"][0][:, cols].rearrange("(c p) n -> p c n", p=P))],
                            (unit_lo, ff_first_unit(s) + 4)))
                    if s >= 1:
                        rows = slice((s - 1) * 256, s * 256)
                        end = ff_first_unit(s) + 6 if s < FF_STEPS else FF_UNITS
                        loads.append((("dn", s - 1), [
                            (0, 2048, 2, a["ffn_w_down"][0][rows, :].rearrange("(c p) n -> p c n", p=P))],
                            (unit_lo, end)))
                    for strip in FF_ADA.get(s, ()):
                        load_ada(*strip[1:])

        place_of, full_at = {}, {}
        filled = [0] * RING
        for n, (name, parts, _) in enumerate(loads):
            filled[n % RING] += 16 * len(parts)
            place_of[name] = n % RING
            full_at[name] = filled[n % RING]
        L0 = len(loads)

        def slot_of(name):
            return raw[:, place_of[name], :]

        def wait_load(eng, name):
            eng.wait_ge(slot_full[place_of[name]], full_at[name])

        def moe_slot(m):
            return (L0 + m) % RING

        def moe_full(i, m):
            k = moe_slot(m)
            nth = sum(1 for q in range(m) if moe_slot(q) == k) + 1
            return i * (16 * (E_LOADS // RING)) + (filled[k] + 16 * nth)

        e_loads = []
        for j in range(E_STEPS + 1):
            if j < E_STEPS:
                e_loads += [("g", j), ("u", j)]
            if j >= 1:
                e_loads.append(("d", j - 1))

        def bank7(use):
            return BANK7.index(use)

        def prm_col(l, what, k=0):
            base = KC + l * PRM_L + {"q": 0, "kv": 2, "mix": 3, "conv": 3 + KC}[what] + k
            return prm[:, base:base + 1]

        block = ctx.enter_context(nc.Block())

        @block.sync
        def _(sp):
            sp.dma_start(prm_rows[0:KC, :], a["c"].rearrange("a (k p) -> (a k) p", p=P)).then_inc(prm_loaded, 16)
            for l in range(L):
                r = KC + l * PRM_L
                for src, rows in ((a["q_norm_g"][l].rearrange("(k p) -> k p", p=P), 2),
                                  (a["kv_norm_g"][l].rearrange("(k p) -> k p", p=P), 1),
                                  (a["mix_norm_g"][l].rearrange("(k p) -> k p", p=P), KC),
                                  (a["conv_w"][l].rearrange("j (k p) -> (j k) p", p=P), 3 * CC)):
                    sp.dma_start(prm_rows[r:r + rows, :], src).then_inc(prm_loaded, 16)
                    r += rows
                sp.dma_start(ada_bias[:, l, :], a["b_ada"][l].rearrange("(k n) -> k n", n=512)).then_inc(prm_loaded, 16)
            sp.dma_start(pos_i[:, :], a["positions"][0].rearrange("(t p) -> p t", p=P),
                          allow_slow_non_contiguous=True).then_inc(prm_loaded, 16)
            for t in range(TT):
                sp.dma_start(x_sb[:, t, :], a["x"][0, t * P:(t + 1) * P, :]).then_inc(x_loaded, 16)
            for n, (name, parts, _) in enumerate(loads):
                if n >= RING:
                    s, value = loads[n - RING][2]
                    sp.wait_ge(s, value)
                for lo, hi, chunks, src in parts:
                    dst = raw[:, n % RING, lo:hi].rearrange("p (c n) -> p c n", c=chunks)
                    sp.dma_start(dst, src).then_inc(slot_full[n % RING], 16)

            def expert_loads(i, e, first):
                for m, (kind, j) in enumerate(e_loads):
                    if first and m < RING:
                        s, value = loads[L0 + m - RING][2]
                        sp.wait_ge(s, value)
                    else:
                        sp.wait_ge(unit_lo, i * E_UNITS + (FF_UNITS + 4 * (m - RING + 1)))
                    if kind == "d":
                        src = a["moe_w_down"][0][bass.ds(e, 1), j * 512:(j + 1) * 512, :]
                        src = src.rearrange("a (c p) n -> p (a c) n", p=P)
                    else:
                        w = a["moe_w_gate"] if kind == "g" else a["moe_w_up"]
                        src = w[0][bass.ds(e, 1), :, j * 512:(j + 1) * 512].rearrange("a (c p) n -> p (a c) n", p=P)
                    k = moe_slot(m)
                    dst = raw[:, k, :].rearrange("p (c n) -> p c n", c=4 if kind == "d" else KC)
                    sp.dma_start(dst, src).then_inc(slot_full[k], 16)

            expert_loads(0, 0, True)
            with sp.Fori(1, E) as e:
                expert_loads(e, e, False)
            sp.wait_ge(plan_ready, 1)
            n_items = sp.value_load(plan_i[0:1, 0:1], min_val=E, max_val=ITEMS)
            for r in range(OVER):
                with sp.If(n_items > E + r):
                    e = sp.value_load(plan_i[0:1, 1 + r:2 + r], min_val=0, max_val=E - 1)
                    expert_loads(E + r, e, False)
            for t in range(TT):
                sp.wait_ge(x_ready, TT * (2 * L - 1) + t + 1)
                sp.dma_start(out[0, t * P:(t + 1) * P, :], x_sb[:, t, :]).then_inc(out_done, 16)
            sp.wait_ge(out_done, 16 * TT)

        @block.gpsimd
        def _(pool):
            pool.memset(ident[:, :], 0.0).then_inc(const_order, 1)
            pool.memset(causal[:, :], 0.0).then_inc(const_order, 1)
            pool.memset(before[:, :], 1.0).then_inc(const_order, 1)
            pool.memset(ones[:, :], 1.0)
            for k in range(HALF):
                pool.memset(freq[:, k:k + 1], float(np.float32(ROPE_BASE) ** np.float32(-2.0 * k / ROPE)))
            pool.memset(eps[:, 0:1], RMS_EPS)
            pool.memset(eps[:, 1:2], LN_EPS)
            pool.memset(eps[:, 2:3], 0.0)
            pool.iota(slot_i[:, :], [[1, P]], base=0, channel_multiplier=0)
            pool.wait_ge(const_order, 3)
            pool.affine_select(out=ident[:, :], in_=ident[:, :], compare_op=ALU.not_equal, fill=1.0,
                               base=0, pattern=[[-1, P]], channel_multiplier=1)
            pool.affine_select(out=causal[:, :], in_=causal[:, :], compare_op=ALU.is_ge, fill=MASKED,
                               base=0, pattern=[[-1, P]], channel_multiplier=1)
            pool.affine_select(out=before[:, :], in_=before[:, :], compare_op=ALU.is_gt, fill=0.0,
                               base=0, pattern=[[1, P]], channel_multiplier=-1).then_inc(consts, 1)

        @block.scalar
        def _(act):
            count = [0]

            def link(ins):
                count[0] += 1
                ins.then_inc(act_order, 1)
                act.wait_ge(act_order, count[0])

            def drain_ada(l, n):
                use = bank7(("ada", l, n))
                act.wait_ge(bank7_full, use + 1)
                vec, half = n // 2, n % 2
                if vec in (2, 5):
                    act.activation((gate1 if vec == 2 else gate2)[:, half * 512:(half + 1) * 512], ps[:, 7, :], ACT.Copy).then_inc(bank7_free, 1)
                else:
                    row = {0: 0, 1: 1, 3: 2, 4: 3}[vec]
                    one = vec in (1, 4)
                    act.activation(modc[:, l, row, 4 * half:4 * half + 4], ps[:, 7, 0:4], ACT.Identity,
                                   bias=ones[:, 0:1] if one else eps[:, 2:3]).then_inc(bank7_free, 1)

            def modulate(v, l, row, last):
                act.wait_ge(bank7_free, bank7(last) + 1)
                for c in (0, 1, 4, 5):
                    act.wait_ge(xt_mm, KC * v + 2 * (c // 2) + 2)
                    act.activation(h_t[:, c, :], ps[:, c // 2, (c % 2) * T:(c % 2) * T + T], ACT.Identity,
                                   scale=modc[:, l, row + 1, c:c + 1], bias=modc[:, l, row, c:c + 1]).then_inc(ht_ready, 1)

            def layer_std(k):
                for t in range(TT):
                    act.wait_ge(var_ready, TT * k + t + 1)
                    act.activation(std[:, t:t + 1], meanvar[:, t, 1:2], ACT.Sqrt, bias=eps[:, 1:2]).then_inc(std_ready, 1)

            act.dma_start(router_w[:, :, :], a["moe_router_w"][0].rearrange("(c p) e -> p c e", p=P)).then_inc(rt_loaded, 16)
            act.dma_start(router_b[:, :], a["moe_router_b"]).then_inc(rt_loaded, 16)

            def ln_rows(k):
                if k >= 1:
                    act.wait_ge(x_ready, TT * k)
                for dst, src in ((ln_g, a[f"ln{k % 2 + 1}_g"]), (ln_b, a[f"ln{k % 2 + 1}_b"])):
                    act.dma_start(dst[:, :], src[k // 2:k // 2 + 1, :].to_broadcast([P, D])).then_inc(ln_loaded, 16)

            ln_rows(0)
            act.wait_ge(consts, 1)
            act.wait_ge(bank7_full, 1)
            link(act.activation(prm[:, :], ps[:, 7, 0:PRM], ACT.Copy))
            act.activation(c_act[:, :], prm[:, 0:KC], ACT.Silu).then_inc(bank7_free, 1)
            act.wait_ge(angles, 1)
            act.activation(trig[:, :, :, :], ang[:, :, :, :], ACT.Sin).then_inc(trig_ready, 1)
            for n in range(4):
                drain_ada(0, n)

            def mixer(l):
                modulate(2 * l, l, 0, ("ada", l, 3))
                for t in range(TT):
                    act.wait_ge(za_mm, TT * l + t + 1)
                    act.activation(v_sb[:, t, 0:Q_LORA], ps[:, 4 + t, 0:Q_LORA], ACT.Square,
                                   accum_out=ssq[:, 0, t:t + 1])
                    act.activation(v_sb[:, t, Q_LORA:Q_LORA + KV_LORA], ps[:, 4 + t, Q_LORA:Q_LORA + KV_LORA], ACT.Square,
                                   accum_out=ssq[:, 1, t:t + 1]).then_inc(ssq_ready, 1)
                act.wait_ge(ssq_ready, TT * (l + 1))
                act.activation(rms[:, 0, :], ssq[:, 0, :], ACT.Sqrt, scale=1.0 / Q_LORA, bias=eps[:, 0:1])
                act.activation(rms[:, 1, :], ssq[:, 1, :], ACT.Sqrt, scale=1.0 / KV_LORA, bias=eps[:, 0:1]).then_inc(rms_ready, 1)
                act.wait_ge(zb_mm, l + 1)
                act.activation(gb_t[:, :, :].rearrange("p c t -> p (c t)"), ps[:, 0:2, :].rearrange("p b n -> p (b n)"),
                               ACT.Copy).then_inc(gb_ready, 1)
                if l == 0:
                    drain_ada(0, 4)
                act.wait_ge(zc_mm, l + 1)
                act.activation(gc_t[:, :, :].rearrange("p c t -> p (c t)"), ps[:, 2:4, :].rearrange("p b n -> p (b n)"),
                               ACT.Copy).then_inc(gc_ready, 1)
                act.wait_ge(znt_mm, l + 1)
                for k in range(2):
                    act.activation(cq_t[:, k, :], ps[:, 4, k * T:(k + 1) * T], ACT.Copy, scale=prm_col(l, "q", k))
                act.activation(ckv_t[:, :], ps[:, 5, 0:T], ACT.Copy, scale=prm_col(l, "kv"))
                act.activation(kr_t[:, :, :].rearrange("p a t -> p (a t)"), ps[:, 6, :], ACT.Copy).then_inc(znt_ready, 1)
                if l == 0:
                    for n in range(5, 9):
                        drain_ada(0, n)
                act.wait_ge(qn_mm, l + 1)
                act.activation(qn_t[:, :, :].rearrange("p c t -> p (c t)"), ps[:, 2:4, :].rearrange("p b n -> p (b n)"),
                               ACT.Copy).then_inc(qn_ready, 1)
                act.wait_ge(v_mm, l + 1)
                act.activation(v_sb[:, :, :], ps[:, 0:2, :], ACT.Copy).then_inc(v_ready, 1)
                act.wait_ge(conv_ready, l + 1)
                act.activation(sq[:, :, :], cv[:, :, :], ACT.Square).then_inc(conv_sq, 1)
                act.wait_ge(bank7_full, bank7(("ssq_conv", l)) + 1)
                act.activation(gstd[:, 0, :], ps[:, 7, 0:TT], ACT.Sqrt, scale=1.0 / D_CONV,
                               bias=eps[:, 0:1]).then_inc(bank7_free, 1)
                for t in range(TT):
                    act.wait_ge(max_ready, TT * l + t + 1)
                    p = p0 if t == 0 else p1
                    for h in range(HEADS):
                        e = act.activation(p[:, h, :], p[:, h, :], ACT.Exp, scale=SCALE, bias=nmx[:, t, h:h + 1],
                                           accum_out=den[:, t, h:h + 1])
                    e.then_inc(exp_ready, 1)
                act.wait_ge(grr_ready, l + 1)
                for t in range(TT):
                    act.wait_ge(yc_mm, TT * l + t + 1)
                    for half, bank in enumerate(((0, 1), (3, 6))[t]):
                        e = act.activation(yv[:, t, half * 512:(half + 1) * 512], ps[:, bank, :], ACT.Copy,
                                           scale=grr[:, 0, t:t + 1])
                    e.then_inc(yc_ready, 1)
                for n in ((9,), (10, 11))[l]:
                    drain_ada(l, n)
                act.wait_ge(pt_mm, 3 * l + 1)
                act.activation(p_t0[:, :, 0:P], ps[:, 0, :].rearrange("p (h q) -> p h q", h=HEADS), ACT.Copy).then_inc(pt_ready, 1)
                act.wait_ge(pt_mm, 3 * l + 3)
                act.activation(p_t1[:, :, :], ps[:, 3, :].rearrange("p (h q) -> p h q", h=HEADS), ACT.Copy).then_inc(pt_ready, 1)
                act.wait_ge(attn_mm, l + 1)
                act.activation(sq[:, 0:2, :], ps[:, 2, :].rearrange("p (h q) -> p h q", h=2), ACT.Square)
                act.activation(sq[:, 2:4, :], ps[:, 4, :].rearrange("p (h q) -> p h q", h=2), ACT.Square).then_inc(attn_sq, 1)
                act.wait_ge(bank7_full, bank7(("ssq_attn", l)) + 1)
                act.activation(gstd[:, 1, :], ps[:, 7, 0:TT], ACT.Sqrt, scale=1.0 / 512,
                               bias=eps[:, 0:1]).then_inc(bank7_free, 1)
                layer_std(2 * l)

            mixer(0)
            modulate(1, 0, 2, ("ada", 0, 9))
            ln_rows(1)
            act.wait_ge(ht_ready, 2 * KC)
            act.activation(h_hi[:, :, :], h_t[:, :, :], ACT.Copy).then_inc(h_hi_ready, 1)

            def ff_silu(s):
                act.wait_ge(unit_used, ff_first_unit(s) + 4)
                if s >= 1:
                    act.wait_ge(hid_done, s)
                act.activation(sil[:, :], ps[:, 0, :], ACT.Silu).then_inc(silu_done, 1)

            def ff_hidt(s):
                act.wait_ge(hidt_mm, s + 1)
                act.activation(hid_hi[:, :], ps[:, 2, :], ACT.Copy).then_inc(hidt_hi, 1)

            def ff_unit(name, lo, u):
                if lo == 0:
                    wait_load(act, name)
                if u >= SRING:
                    act.wait_ge(unit_used, u - SRING + 1)
                act.activation(w_hi[:, u % SRING, :], slot_of(name)[:, lo:lo + UNIT], ACT.Copy).then_inc(unit_hi, 1)

            for s in range(FF_STEPS + 1):
                u = ff_first_unit(s)
                if s < FF_STEPS:
                    for k in range(4):
                        ff_unit(("gu", s), k * UNIT, u + k)
                    if s >= 1:
                        ff_hidt(s - 1)
                        for strip in FF_ADA[s - 1]:
                            drain_ada(*strip[1:])
                    u += 4
                if s >= 1:
                    for k in range(2):
                        ff_unit(("dn", s - 1), k * UNIT, u + k)
                if s == FF_STEPS:
                    ff_hidt(s - 1)
                    for strip in FF_ADA[s - 1]:
                        drain_ada(*strip[1:])
                if s < FF_STEPS:
                    ff_silu(s)
            layer_std(1)

            ln_rows(2)
            mixer(1)
            modulate(3, 1, 2, ("ada", 1, 9))
            ln_rows(3)

            def moe_hi(i, k):
                m = k // 4
                if k % 4 == 0:
                    act.wait_ge(slot_full[moe_slot(m)], moe_full(i, m))
                act.wait_ge(unit_used, i * E_UNITS + (FF_UNITS + k - SRING + 1))
                act.activation(w_hi[:, (FF_UNITS + k) % SRING, :],
                               raw[:, moe_slot(m), (k % 4) * UNIT:(k % 4 + 1) * UNIT], ACT.Copy).then_inc(unit_hi, 1)

            for k in range(HEAD):
                moe_hi(0, k)
            act.wait_ge(rel_ready, 1)
            act.activation(expo[:, :, :], expo[:, :, :], ACT.Exp).then_inc(expo_ready, 1)

            def gathered(i):
                act.wait_ge(xg_mm, i + 1)
                for c in range(KC // 2):
                    e = act.activation(xg[:, c, :], ps[:, 5, c * P:(c + 1) * P], ACT.Identity,
                                       scale=modc[:, 1, 3, c:c + 1], bias=modc[:, 1, 2, c:c + 1])
                e.then_inc(xg_ready, 1)
                act.wait_ge(xg_ready, i + 1)
                act.activation(xg_hi[:, 0:KC // 2, :], xg[:, 0:KC // 2, :], ACT.Copy).then_inc(xg_hi_ready, 1)

            gathered(0)

            def item(i, head, tail):
                after = {}
                for j in range(E_STEPS):
                    after.setdefault(moe_first_unit(j) + 6, []).append(("silu", j))
                    after.setdefault(moe_first_unit(j + 1) + 5 if j < E_STEPS - 1 else E_UNITS - 3, []).append(("hidt", j))
                for k in range(HEAD if head else 0, E_UNITS):
                    moe_hi(i, k)
                    for what, j in after.get(k, ()):
                        if what == "silu":
                            act.wait_ge(unit_used, i * E_UNITS + (FF_UNITS + moe_first_unit(j) + 4))
                            act.wait_ge(hid_done, i * E_STEPS + (FF_STEPS + j))
                            act.activation(sil[:, :], ps[:, GATE_BANKS[j % 2], :], ACT.Silu).then_inc(silu_done, 1)
                        else:
                            act.wait_ge(hidt_mm, i * E_STEPS + (FF_STEPS + j + 1))
                            act.activation(hid_hi[:, :], ps[:, 2, :], ACT.Copy).then_inc(hidt_hi, 1)
                gathered(i + 1)
                if tail:
                    moe_hi(i + 1, 0)
                    moe_hi(i + 1, 1)
                act.wait_ge(unit_used, i * E_UNITS + (FF_UNITS + E_UNITS))
                act.activation(y_sb[:, 0:512], ps[:, 3, :], ACT.Copy).then_inc(y_ready, 1)
                if tail:
                    moe_hi(i + 1, 2)

            with act.Fori(0, E - 1) as i:
                item(i, True, True)
            item(E - 1, True, False)
            act.wait_ge(plan_ready, 1)
            n_items = act.value_load(plan_i[0:1, 0:1], min_val=E, max_val=ITEMS)
            for r in range(OVER):
                with act.If(n_items > E + r):
                    item(E + r, False, False)
            layer_std(3)

        @block.vector
        def _(dve):
            count = [0]

            def link(ins):
                count[0] += 1
                ins.then_inc(dve_order, 1)
                dve.wait_ge(dve_order, count[0])

            def ada(l, n):
                k = ADA_ORDER.index(("ada", l, n))
                wait_load(dve, ("ada", l, n))
                if k >= 2:
                    dve.wait_ge(bank7_full, bank7(ADA_ORDER[k - 2]) + 1)
                w = slot_of(("ada", l, n)).rearrange("p (c n) -> p c n", c=KC)
                acc = ada_acc[:, k % 2, :]
                link(dve.tensor_scalar(acc, w[:, 0, :], c_act[:, 0:1], None, ALU.mult))
                for c in range(1, KC):
                    ins = dve.scalar_tensor_tensor(acc, w[:, c, :], c_act[:, c:c + 1], acc, ALU.mult, ALU.add)
                    if c < KC - 1:
                        link(ins)
                ins.then_inc(ada_summed, 1)

            def modulate(v, l, row, last):
                dve.wait_ge(bank7_free, bank7(last) + 1)
                for c in (2, 3, 6, 7):
                    dve.wait_ge(xt_mm, KC * v + 2 * (c // 2) + 2)
                    dve.tensor_scalar(h_t[:, c, :], ps[:, c // 2, (c % 2) * T:(c % 2) * T + T],
                                      modc[:, l, row + 1, c:c + 1], modc[:, l, row, c:c + 1], ALU.mult,
                                      ALU.add).then_inc(ht_ready, 1)

            def layer_norm(k, t, gated):
                y = yv[:, t, :]
                gated(t)
                link(dve.scalar_tensor_tensor(y, x_sb[:, t, :], ALPHA, y, ALU.mult, ALU.add))
                for half in range(2):
                    ins = dve.bn_stats(stats[:, t, half, :], yv[:, t, half * 512:(half + 1) * 512])
                link(ins)
                dve.bn_aggr(meanvar[:, t, :], stats[:, t, :, :]).then_inc(var_ready, 1)
                dve.wait_ge(var_ready, TT * k + t + 1)
                dve.wait_ge(std_ready, TT * k + t + 1)
                link(dve.reciprocal(rstd[:, t:t + 1], std[:, t:t + 1]))
                link(dve.tensor_scalar(y, y, meanvar[:, t, 0:1], rstd[:, t:t + 1], ALU.subtract, ALU.mult))
                dve.wait_ge(ln_loaded, 32 * (k + 1))
                link(dve.tensor_tensor(y, y, ln_g[:, :], ALU.mult))
                dve.tensor_tensor(x_sb[:, t, :], y, ln_b[:, :], ALU.add).then_inc(x_ready, 1)

            dve.memset(cu[:, :, 0:2], 0.0)
            dve.wait_ge(consts, 1)
            dve.wait_ge(prm_loaded, 16 * (2 + 5 * L))
            dve.tensor_copy(slot_no[:, :], slot_i[:, :])
            link(dve.tensor_copy(pos_f[:, :], pos_i[:, :]))
            for t in range(TT):
                for k in range(2):
                    ins = dve.tensor_scalar(ang[:, k, t, :], freq[:, :], pos_f[:, t:t + 1], None, ALU.mult)
            link(ins)
            link(dve.tensor_scalar(turns[:, 0], ang[:, 0], 1.0 / TWO_PI, 0.25, ALU.mult, ALU.add))
            link(dve.tensor_scalar(turns[:, 1], ang[:, 1], 1.0 / TWO_PI, None, ALU.mult))
            magic = 1.5 * 2.0 ** 23
            link(dve.tensor_scalar(turns[:], turns[:], magic, None, ALU.add))
            link(dve.tensor_scalar(turns[:], turns[:], -magic, None, ALU.add))
            for part in split2pi():
                link(dve.scalar_tensor_tensor(ang[:], turns[:], -part, ang[:], ALU.mult, ALU.add))
            link(dve.tensor_scalar(ang[:, 0], ang[:, 0], float(np.pi / 2), None, ALU.add))
            dve.tensor_scalar(ang[:], ang[:], 3.1415925, -3.1415925, ALU.min, ALU.max).then_inc(angles, 1)
            dve.wait_ge(bank7_free, 1)
            for n in range(4):
                ada(0, n)

            def rotate(dst1, dst2, x1, x2, cos, sin, tmp):
                dve.tensor_tensor(tmp[0], x1, cos, ALU.mult)
                dve.tensor_tensor(tmp[1], x2, sin, ALU.mult)
                dve.tensor_tensor(tmp[2], x2, cos, ALU.mult)
                link(dve.tensor_tensor(tmp[3], x1, sin, ALU.mult))
                dve.tensor_tensor(dst1, tmp[0], tmp[1], ALU.subtract)
                return dve.tensor_tensor(dst2, tmp[2], tmp[3], ALU.add)

            def mixer(l):
                modulate(2 * l, l, 0, ("ada", l, 3))
                dve.wait_ge(rms_ready, l + 1)
                link(dve.reciprocal(rrms[:, :, :], rms[:, :, :]))
                for t in range(TT):
                    dve.tensor_scalar(zn[:, t, 0:Q_LORA], ps[:, 4 + t, 0:Q_LORA], rrms[:, 0, t:t + 1], None, ALU.mult)
                    dve.tensor_scalar(zn[:, t, Q_LORA:], ps[:, 4 + t, Q_LORA:Q_LORA + KV_LORA],
                                      rrms[:, 1, t:t + 1], None, ALU.mult)
                if l == 0:
                    dve.wait_ge(trig_ready, 1)
                k0 = Q_LORA + KV_LORA
                link(dve.memset(kr[:, :, :, :, :], 0.0))
                link(rotate(kr[:, :, 0, 0, 0:HALF], kr[:, :, 0, 0, HALF:], ps[:, 4:6, k0:k0 + HALF],
                            ps[:, 4:6, k0 + HALF:k0 + ROPE], trig[:, 0], trig[:, 1], [rp_k[:, k] for k in range(4)]))
                dve.tensor_copy(kr[:, :, 1, 1, :], kr[:, :, 0, 0, :]).then_inc(zn_ready, 1)
                if l == 0:
                    for n in range(4, 9):
                        ada(0, n)
                dve.wait_ge(zu_mm, l + 1)
                dve.wait_ge(gc_ready, l + 1)
                dve.tensor_tensor(cu[:, :, 2:], ps[:, 0:2, :].rearrange("p b (c t) -> p (b c) t", c=2), gc_t[:, :, :],
                                  ALU.mult).then_inc(cu_ready, 1)
                dve.wait_ge(kn_mm, l + 1)
                dve.tensor_copy(kn_t[:, :, :].rearrange("p c t -> p (c t)"),
                                ps[:, 4:6, :].rearrange("p b n -> p (b n)")).then_inc(kn_ready, 1)
                dve.wait_ge(qr_mm, l + 1)
                q = ps[:, 6, :].rearrange("p (t h r) -> p t h r", t=TT, h=HEADS)
                for t in range(TT):
                    cos = trig[:, 0, t:t + 1, :].to_broadcast([P, HEADS, HALF])
                    sin = trig[:, 1, t:t + 1, :].to_broadcast([P, HEADS, HALF])
                    ins = rotate(qr[:, t, :, 0:HALF], qr[:, t, :, HALF:], q[:, t, :, 0:HALF], q[:, t, :, HALF:],
                                 cos, sin, [rp_q[:, k, t] for k in range(4)])
                ins.then_inc(qr_ready, 1)
                dve.wait_ge(cu_ready, l + 1)
                dve.wait_ge(qr_ready, l + 1)
                for c in range(CC):
                    dve.tensor_scalar(cv[:, c, :], cu[:, c, 2:], prm_col(l, "conv", 2 * CC + c), None, ALU.mult).then_inc(dve_order, 1)
                count[0] += CC
                for j in (1, 0):
                    dve.wait_ge(dve_order, count[0])
                    for c in range(CC):
                        dve.scalar_tensor_tensor(cv[:, c, :], cu[:, c, j:j + T], prm_col(l, "conv", j * CC + c),
                                                 cv[:, c, :], ALU.mult, ALU.add).then_inc(dve_order, 1)
                    count[0] += CC
                dve.wait_ge(dve_order, count[0])
                dve.wait_ge(gb_ready, l + 1)
                dve.tensor_tensor(cv[:, :, :], cv[:, :, :], gb_t[:, :, :], ALU.mult).then_inc(conv_ready, 1)
                dve.wait_ge(qrt_mm, l + 1)
                dve.tensor_copy(qr_t[:, :, :].rearrange("p c t -> p (c t)"), ps[:, 6, :]).then_inc(qrt_ready, 1)
                dve.wait_ge(conv_ready, l + 1)
                for c in range(CC):
                    ins = dve.tensor_scalar(cv_t[:, c, :], cv[:, c, :], prm_col(l, "mix", 4 + c), None, ALU.mult)
                ins.then_inc(conv_scaled, 1)
                for n in ((9,), (10, 11))[l]:
                    ada(l, n)
                dve.wait_ge(score_mm, TT * l + 1)
                mask = causal[:, :].rearrange("p (a s) -> p a s", a=1).to_broadcast([P, HEADS, P])
                link(dve.tensor_tensor(p0[:, :, :], ps[:, 2, :].rearrange("p (h s) -> p h s", h=HEADS), mask, ALU.add))
                link(dve.tensor_reduce(mx[:, 0, :], p0[:, :, :], AX_X, ALU.max))
                dve.tensor_scalar(nmx[:, 0, :], mx[:, 0, :], -SCALE, None, ALU.mult).then_inc(max_ready, 1)
                dve.wait_ge(score_mm, TT * l + 2)
                s1 = ps[:, 4:6, :].rearrange("p b (h s) -> p (b h) s", h=2)
                dve.tensor_copy(p1[:, :, 0:P], s1[:, :, 0:P])
                link(dve.tensor_tensor(p1[:, :, P:T], s1[:, :, P:T], mask, ALU.add))
                link(dve.tensor_reduce(mx[:, 1, :], p1[:, :, :], AX_X, ALU.max))
                dve.tensor_scalar(nmx[:, 1, :], mx[:, 1, :], -SCALE, None, ALU.mult).then_inc(max_ready, 1)
                dve.wait_ge(bank7_free, bank7(("ssq_conv", l)) + 1)
                dve.reciprocal(grr[:, 0, :], gstd[:, 0, :]).then_inc(grr_ready, 1)
                for t in range(TT):
                    dve.wait_ge(exp_ready, TT * l + t + 1)
                    link(dve.reciprocal(rden[:, t, :], den[:, t, :]))
                    p = p0 if t == 0 else p1
                    for h in range(HEADS):
                        ins = dve.tensor_scalar(p[:, h, :], p[:, h, :], rden[:, t, h:h + 1], None, ALU.mult)
                    ins.then_inc(prob_ready, 1)
                dve.wait_ge(pt_mm, 3 * l + 2)
                dve.tensor_copy(p_t0[:, :, P:T], ps[:, 1, :].rearrange("p (h q) -> p h q", h=HEADS)).then_inc(pt_ready, 1)
                dve.wait_ge(attn_mm, l + 1)
                dve.wait_ge(attn_sq, l + 1)
                for h in range(HEADS):
                    ins = dve.tensor_scalar(a_t[:, h, :], ps[:, 2 + 2 * (h // 2), (h % 2) * T:(h % 2 + 1) * T],
                                            prm_col(l, "mix", h), None, ALU.mult)
                ins.then_inc(attn_scaled, 1)
                dve.wait_ge(bank7_free, bank7(("ssq_attn", l)) + 1)
                link(dve.reciprocal(grr[:, 1, :], gstd[:, 1, :]))
                dve.wait_ge(yc_ready, TT * (l + 1))
                dve.wait_ge(bank7_free, bank7(("ada", l, 5)) + 1)

                def gated(t):
                    dve.wait_ge(ya_mm, TT * l + t + 1)
                    b = (0, 5)[t]
                    link(dve.scalar_tensor_tensor(yv[:, t, :], ps[:, b:b + 2, :].rearrange("p b n -> p (b n)"),
                                                  grr[:, 1, t:t + 1], yv[:, t, :], ALU.mult, ALU.add))
                    link(dve.tensor_tensor(yv[:, t, :], yv[:, t, :], gate1[:, :], ALU.mult))

                for t in range(TT):
                    layer_norm(2 * l, t, gated)

            dve.wait_ge(x_loaded, 16 * TT)
            mixer(0)
            modulate(1, 0, 2, ("ada", 0, 9))
            dve.wait_ge(h_hi_ready, 1)
            dve.tensor_tensor(h_lo[:, :, :], h_t[:, :, :], h_hi[:, :, :].bitcast(F32), ALU.subtract).then_inc(h_lo_ready, 1)

            def ff_unit(name, lo, u):
                dve.wait_ge(unit_hi, u + 1)
                dve.tensor_tensor(w_lo[:, u % SRING, :], slot_of(name)[:, lo:lo + UNIT],
                                  w_hi[:, u % SRING, :].bitcast(F32), ALU.subtract).then_inc(unit_lo, 1)

            def hidden(n):
                dve.wait_ge(silu_done, n + 1)
                dve.tensor_tensor(hid, ps[:, 1, :].rearrange("p (f n) -> p f n", f=4),
                                  sil[:, :].rearrange("p (f n) -> p f n", f=4), ALU.mult).then_inc(hid_done, 1)

            def hidden_lo(n):
                dve.wait_ge(hidt_hi, n + 1)
                dve.tensor_tensor(hid_lo[:, :], ps[:, 2, :], hid_hi[:, :].bitcast(F32), ALU.subtract).then_inc(hidt_lo, 1)

            for s in range(FF_STEPS + 1):
                u = ff_first_unit(s)
                if s < FF_STEPS:
                    for k in range(4):
                        ff_unit(("gu", s), k * UNIT, u + k)
                    if s >= 1:
                        hidden_lo(s - 1)
                    u += 4
                if s >= 1:
                    for k in range(2):
                        ff_unit(("dn", s - 1), k * UNIT, u + k)
                if s < FF_STEPS:
                    if s >= 1:
                        dve.wait_ge(hidt_mm, s)
                    hidden(s)
                else:
                    hidden_lo(s - 1)
                for strip in FF_ADA.get(s, ()):
                    ada(*strip[1:])

            dve.wait_ge(unit_used, FF_UNITS)
            dve.wait_ge(bank7_free, bank7(("ada", 0, 11)) + 1)

            def gated_ff(t):
                link(dve.tensor_tensor(yv[:, t, :], ps[:, 3 + 2 * t:5 + 2 * t, :].rearrange("p b n -> p (b n)"),
                                       gate2[:, :], ALU.mult))

            for t in range(TT):
                layer_norm(1, t, gated_ff)

            dve.memset(cu[:, :, 0:2], 0.0)
            mixer(1)
            modulate(3, 1, 2, ("ada", 1, 9))

            for ap in (pads[:], cnt[:]):
                dve.memset(ap, 0.0)
            dve.memset(place[:, :, ITEMS:], -1.0)
            dve.memset(share[:, :, ITEMS:], 0.0)
            dve.tensor_copy(e_no[:, :], slot_no[:, 0:E])
            link(dve.memset(moe_acc[:, :, :], 0.0))
            dve.wait_ge(logit_mm, 1)
            link(dve.tensor_copy(logit[:, :, :], ps[:, 4, 0:TT * E].rearrange("p (t e) -> p t e", t=TT)))
            for t in range(TT):
                ins = dve.max(top[:, t, :], logit[:, t, :])
            link(ins)
            for t in range(TT):
                dve.tensor_scalar(expo[:, t, :], logit[:, t, :], top[:, t, 0:1], None, ALU.subtract).then_inc(rel_ready, 1) \
                    if t == TT - 1 else dve.tensor_scalar(expo[:, t, :], logit[:, t, :], top[:, t, 0:1], None, ALU.subtract)
                dve.tensor_scalar(above[:, t, :], logit[:, t, :], top[:, t, 1:2], None, ALU.is_gt)
                ins = dve.tensor_scalar(pads[:, 0, t, E:], logit[:, t, :], top[:, t, 1:2], None, ALU.is_equal)
            link(ins)

            def prefix(p, q, r, shape_of):
                link(dve.tensor_tensor(shape_of(q, 0), shape_of(p, 0), shape_of(p, 1), ALU.add))
                link(dve.tensor_tensor(shape_of(r, 0), shape_of(q, 0), shape_of(q, 2), ALU.add))
                link(dve.tensor_tensor(shape_of(q, 0), shape_of(r, 0), shape_of(r, 4), ALU.add))

            prefix(0, 1, 2, lambda k, back: pads[:, k, :, E - back:2 * E - back])
            link(dve.tensor_reduce(n_above[:, :], above[:, :, :], AX_X, ALU.add))
            link(dve.tensor_scalar(n_above[:, :], n_above[:, :], -1.0, 2.0, ALU.mult, ALU.add))
            for t in range(TT):
                ins = dve.scalar_tensor_tensor(chosen[:, t, :], pads[:, 1, t, E:], n_above[:, t:t + 1],
                                               pads[:, 0, t, E:], ALU.is_le, ALU.mult)
            link(ins)
            dve.tensor_tensor(chosen[:, :, :], chosen[:, :, :], above[:, :, :], ALU.add).then_inc(chosen_ready, 1)
            dve.wait_ge(chosen_ready, 1)
            dve.wait_ge(expo_ready, 1)
            link(dve.tensor_tensor(expo[:, :, :], expo[:, :, :], chosen[:, :, :], ALU.mult))
            link(dve.tensor_reduce(exsum[:, :], expo[:, :, :], AX_X, ALU.add))
            link(dve.reciprocal(exinv[:, :], exsum[:, :]))
            for t in range(TT):
                ins = dve.tensor_scalar(share[:, t, 0:E], expo[:, t, :], exinv[:, t:t + 1], None, ALU.mult)
            link(ins)
            dve.wait_ge(place_mm, 1)
            pos = ps[:, 4, 64:64 + TT * E].rearrange("p (t e) -> p t e", t=TT)
            link(dve.scalar_tensor_tensor(place[:, :, 0:E], pos, 1.0, chosen[:, :, :], ALU.add, ALU.mult))
            link(dve.tensor_scalar(place[:, :, 0:E], place[:, :, 0:E], -1.0, None, ALU.add))

            def build_sel(i):
                for t in range(TT):
                    ins = dve.tensor_scalar(sel[:, t, :], slot_no[:, :], place[:, t, bass.ds(i, 1)], None, ALU.is_equal)
                ins.then_inc(sel_ready, 1)

            link(dve.tensor_scalar(cnt[:, 0, E:], ps[:, 4, 64 + TT * E:64 + TT * E + E], float(P), None, ALU.is_gt))
            build_sel(0)
            prefix(0, 1, 2, lambda k, back: cnt[:, k, E - back:2 * E - back])
            link(dve.tensor_tensor(rank[:, :], cnt[:, 1, E:], cnt[:, 0, E:], ALU.subtract))
            for r in range(OVER):
                ins = dve.scalar_tensor_tensor(pick[:, r, :], rank[:, :], float(r), cnt[:, 0, E:], ALU.is_equal, ALU.mult)
            link(ins)
            for r in range(OVER):
                for t in range(TT):
                    dve.scalar_tensor_tensor(picked[:, r, t, :], place[:, t, 0:E], float(1 - P), pick[:, r, :],
                                             ALU.add, ALU.mult)
                    dve.tensor_tensor(picked[:, r, TT + t, :], share[:, t, 0:E], pick[:, r, :], ALU.mult)
                ins = dve.tensor_tensor(picked[:, r, 4, :], e_no[:, :], pick[:, r, :], ALU.mult)
            link(ins)
            for r in range(OVER):
                for t in range(TT):
                    dve.tensor_reduce(place[:, t, E + r:E + r + 1], picked[:, r, t, :], AX_X, ALU.add)
                    dve.tensor_reduce(share[:, t, E + r:E + r + 1], picked[:, r, TT + t, :], AX_X, ALU.add)
                dve.tensor_reduce(plan_f[:, 1 + r:2 + r], picked[:, r, 4, :], AX_X, ALU.add)
            link(dve.tensor_reduce(plan_f[:, 0:1], cnt[:, 0, E:], AX_X, ALU.add))
            link(dve.tensor_scalar(place[:, :, E:ITEMS], place[:, :, E:ITEMS], -1.0, None, ALU.add))
            link(dve.tensor_scalar(plan_f[:, 0:1], plan_f[:, 0:1], float(E), None, ALU.add))
            dve.tensor_copy(plan_i[:, :], plan_f[:, :]).then_inc(plan_ready, 1)

            def gathered(i):
                half = slice(KC // 2, KC)
                dve.wait_ge(xg_mm, i + 1)
                for c in range(KC // 2, KC):
                    ins = dve.tensor_scalar(xg[:, c, :], ps[:, 6, (c - 4) * P:(c - 3) * P], modc[:, 1, 3, c:c + 1],
                                            modc[:, 1, 2, c:c + 1], ALU.mult, ALU.add)
                ins.then_inc(xg2_ready, 1)
                dve.wait_ge(xg2_ready, i + 1)
                dve.tensor_copy(xg_hi[:, half, :], xg[:, half, :]).then_inc(xg2_hi, 1)
                dve.wait_ge(xg2_hi, i + 1)
                dve.tensor_tensor(xg_lo[:, half, :], xg[:, half, :], xg_hi[:, half, :].bitcast(F32), ALU.subtract)
                dve.wait_ge(xg_hi_ready, i + 1)
                half = slice(0, KC // 2)
                dve.tensor_tensor(xg_lo[:, half, :], xg[:, half, :], xg_hi[:, half, :].bitcast(F32),
                                  ALU.subtract).then_inc(xg_lo_ready, 1)

            def moe_lo(i, k):
                m = k // 4
                q = (FF_UNITS + k) % SRING
                dve.wait_ge(unit_hi, i * E_UNITS + (FF_UNITS + k + 1))
                dve.tensor_tensor(w_lo[:, q, :], raw[:, moe_slot(m), (k % 4) * UNIT:(k % 4 + 1) * UNIT],
                                  w_hi[:, q, :].bitcast(F32), ALU.subtract).then_inc(unit_lo, 1)

            for k in range(HEAD):
                moe_lo(0, k)
            gathered(0)
            dve.wait_ge(plan_ready, 1)

            def item(i, head, tail):
                after = {}
                for j in range(E_STEPS):
                    after.setdefault(moe_first_unit(j) + 9, []).append(("hid", j))
                    after.setdefault(moe_first_unit(j + 1) + 5 if j < E_STEPS - 1 else E_UNITS - 3, []).append(("hidt", j))
                for k in range(HEAD if head else 0, E_UNITS):
                    moe_lo(i, k)
                    for what, j in after.get(k, ()):
                        if what == "hid":
                            dve.wait_ge(unit_used, i * E_UNITS + (FF_UNITS + moe_first_unit(j) + 8))
                            dve.wait_ge(hidt_mm, i * E_STEPS + (FF_STEPS + j))
                            hidden(i * E_STEPS + (FF_STEPS + j))
                        else:
                            hidden_lo(i * E_STEPS + (FF_STEPS + j))
                    if k == 16:
                        dve.wait_ge(selt_mm, i + 1)
                        dve.tensor_copy(sel_t, ps[:, 5, 0:T].rearrange("p (t n) -> p t n", t=TT)).then_inc(selt_ready, 1)
                        build_sel(i + 1)
                gathered(i + 1)
                if tail:
                    moe_lo(i + 1, 0)
                    moe_lo(i + 1, 1)
                dve.wait_ge(unit_used, i * E_UNITS + (FF_UNITS + E_UNITS))
                dve.tensor_copy(y_sb[:, 512:], ps[:, 4, :]).then_inc(y2_ready, 1)
                if tail:
                    moe_lo(i + 1, 2)
                for half in range(2):
                    for t in range(TT):
                        dve.wait_ge(scatter_mm, i * 4 + (2 * half + t + 1))
                        dve.wait_ge(acc_ready, i * 4 + 1)
                        acc = moe_acc[:, t, half * 512:(half + 1) * 512]
                        dve.scalar_tensor_tensor(acc, ps[:, SCATTER_BANKS[t][half], :], share[:, t, bass.ds(i, 1)], acc,
                                                 ALU.mult, ALU.add).then_inc(acc_ready, 1)

            dve.memset(n_above[:, :], 0.0).then_inc(acc_ready, 1)
            with dve.Fori(0, E - 1) as i:
                item(i, True, True)
            item(E - 1, True, False)
            n_items = dve.value_load(plan_i[0:1, 0:1], min_val=E, max_val=ITEMS)
            for r in range(OVER):
                with dve.If(n_items > E + r):
                    item(E + r, False, False)
            link(dve.memset(n_above[:, :], 0.0))
            dve.wait_ge(bank7_free, bank7(("ada", 1, 11)) + 1)

            def gated_moe(t):
                link(dve.tensor_tensor(yv[:, t, :], moe_acc[:, t, :], gate2[:, :], ALU.mult))

            for t in range(TT):
                layer_norm(3, t, gated_moe)

        @block.tensor
        def _(pe):
            def use_bank7(use):
                k = bank7(use)
                if k >= 1:
                    pe.wait_ge(bank7_free, k)

            def ada(l, n):
                k = ADA_ORDER.index(("ada", l, n))
                pe.wait_ge(ada_summed, k + 1)
                use_bank7(("ada", l, n))
                acc = ada_acc[:, k % 2, :]
                if n // 2 in (2, 5):
                    pe.matmul(ps[:, 7, :], ones[:, :], acc, start=True, stop=False)
                    m = pe.matmul(ps[:, 7, :], ident[0:STRIPS, n:n + 1].to_broadcast([STRIPS, P]),
                                  ada_bias[:, l, :], start=False, stop=True)
                else:
                    for c in range(4):
                        cols = slice(c * P, (c + 1) * P)
                        pe.matmul(ps[:, 7, c:c + 1], acc[:, cols], ones[:, 0:1], start=True, stop=False)
                        m = pe.matmul(ps[:, 7, c:c + 1], ada_bias[:, l, cols], ident[0:STRIPS, n:n + 1],
                                      start=False, stop=True)
                m.then_inc(bank7_full, 1)

            def turn_input(v):
                if v >= 1:
                    pe.wait_ge(x_ready, TT * v)
                else:
                    pe.wait_ge(x_loaded, 16 * TT)
                for c in range(KC):
                    for t in range(TT):
                        o = (c % 2) * T + t * P
                        m = pe.transpose(ps[:, c // 2, o:o + P], x_sb[:, t, c * P:(c + 1) * P], ident[:, :])
                    m.then_inc(xt_mm, 1)

            pe.wait_ge(consts, 1)
            pe.wait_ge(prm_loaded, 16 * (2 + 5 * L))
            pe.transpose(ps[:, 7, 0:PRM], prm_rows[:, :], ident[0:PRM, 0:PRM]).then_inc(bank7_full, 1)
            for n in range(4):
                ada(0, n)

            def mixer(l):
                turn_input(2 * l)
                wait_load(pe, ("wa", l))
                pe.wait_ge(ht_ready, KC * (2 * l + 1))
                wa = slot_of(("wa", l))[:, 0:KC * ZA].rearrange("p (c n) -> p c n", c=KC)
                for t in range(TT):
                    for c in range(KC):
                        m = pe.matmul(ps[:, 4 + t, 0:ZA], h_t[:, c, t * P:(t + 1) * P], wa[:, c, :],
                                      start=(c == 0), stop=(c == KC - 1))
                    m.then_inc(za_mm, 1)

                def channels(name, bank):
                    wait_load(pe, name)
                    w = slot_of(name).rearrange("p (c n) -> p c n", c=KC)
                    for n in range(CC):
                        for c in range(KC):
                            m = pe.matmul(ps[:, bank + n // 2, (n % 2) * T:(n % 2 + 1) * T],
                                          w[:, c, n * P:(n + 1) * P], h_t[:, c, :], start=(c == 0), stop=(c == KC - 1))
                    return m

                channels(("wb", l), 0).then_inc(zb_mm, 1)
                if l == 0:
                    ada(0, 4)
                channels(("wc", l), 2).then_inc(zc_mm, 1)
                pe.wait_ge(zn_ready, l + 1)
                for k in range(2):
                    for t in range(TT):
                        pe.transpose(ps[:, 4, k * T + t * P:k * T + (t + 1) * P], zn[:, t, k * P:(k + 1) * P], ident[:, :])
                for t in range(TT):
                    pe.transpose(ps[:, 5, t * P:(t + 1) * P], zn[:, t, Q_LORA:], ident[:, :])
                    for k in range(2):
                        m = pe.transpose(ps[:, 6, k * T + t * P:k * T + (t + 1) * P],
                                         kr[:, t, k, :, :].rearrange("p a r -> p (a r)"), ident[:, :])
                m.then_inc(znt_mm, 1)
                if l == 0:
                    ada(0, 5)
                    ada(0, 6)
                pe.wait_ge(gb_ready, l + 1)
                channels(("wu", l), 0).then_inc(zu_mm, 1)
                if l == 0:
                    ada(0, 7)
                    ada(0, 8)
                wait_load(pe, ("qkv", l))
                uq = slot_of(("qkv", l))[:, 0:2 * 768].rearrange("p (c h n) -> p c h n", c=2, h=HEADS)
                ukv = slot_of(("qkv", l))[:, 2 * 768:2 * 768 + 1024].rearrange("p (h n) -> p h n", h=HEADS)
                pe.wait_ge(znt_ready, l + 1)
                pe.wait_ge(gc_ready, l + 1)
                for h in range(HEADS):
                    for c in range(2):
                        m = pe.matmul(ps[:, 2 + h // 2, (h % 2) * T:(h % 2 + 1) * T], uq[:, c, h, 0:NOPE], cq_t[:, c, :],
                                      start=(c == 0), stop=(c == 1))
                m.then_inc(qn_mm, 1)
                for h in range(HEADS):
                    m = pe.matmul(ps[:, 4 + h // 2, (h % 2) * T:(h % 2 + 1) * T], ukv[:, h, 0:NOPE], ckv_t[:, :],
                                  start=True, stop=True)
                m.then_inc(kn_mm, 1)
                for t in range(TT):
                    for c in range(2):
                        m = pe.matmul(ps[:, 6, t * T:(t + 1) * T], cq_t[:, c, t * P:(t + 1) * P], uq[:, c, :, NOPE:],
                                      start=(c == 0), stop=(c == 1))
                m.then_inc(qr_mm, 1)
                pe.wait_ge(cu_ready, l + 1)
                for t in range(TT):
                    m = pe.matmul(ps[:, t, :], ckv_t[:, t * P:(t + 1) * P], ukv[:, :, NOPE:], start=True, stop=True)
                m.then_inc(v_mm, 1)
                pe.wait_ge(qr_ready, l + 1)
                for k in range(2):
                    for t in range(TT):
                        m = pe.transpose(ps[:, 6, k * T + t * P:k * T + (t + 1) * P],
                                         qr[:, t, 2 * k:2 * k + 2, :].rearrange("p h r -> p (h r)"), ident[:, :])
                m.then_inc(qrt_mm, 1)
                pe.wait_ge(qn_ready, l + 1)
                pe.wait_ge(kn_ready, l + 1)
                pe.wait_ge(qrt_ready, l + 1)
                for t in range(TT):
                    keys = P * (t + 1)
                    for h in range(HEADS):
                        o = ps[:, 2, h * P:(h + 1) * P] if t == 0 else ps[:, 4 + h // 2, (h % 2) * T:(h % 2 + 1) * T]
                        pe.matmul(o, qn_t[:, h, t * P:(t + 1) * P], kn_t[:, h, 0:keys], start=True, stop=False)
                        m = pe.matmul(o, qr_t[:, h // 2, t * P:(t + 1) * P], kr_t[:, h % 2, 0:keys],
                                      start=False, stop=True)
                    m.then_inc(score_mm, 1)
                pe.wait_ge(conv_sq, l + 1)
                use_bank7(("ssq_conv", l))
                for t in range(TT):
                    for c in range(CC):
                        m = pe.matmul(ps[:, 7, t:t + 1], sq[:, c, t * P:(t + 1) * P], ones[:, 0:1],
                                      start=(c == 0), stop=(c == CC - 1))
                m.then_inc(bank7_full, 1)
                pe.wait_ge(conv_scaled, l + 1)
                pe.wait_ge(v_ready, l + 1)
                wait_load(pe, ("oc", l))
                oc = slot_of(("oc", l)).rearrange("p (c n) -> p c n", c=4)
                for t in range(TT):
                    for half, bank in enumerate(((0, 1), (3, 6))[t]):
                        for c in range(CC):
                            m = pe.matmul(ps[:, bank, :], cv_t[:, c, t * P:(t + 1) * P], oc[:, c, half * 512:(half + 1) * 512],
                                          start=(c == 0), stop=(c == CC - 1))
                    m.then_inc(yc_mm, 1)
                for n in ((9,), (10, 11))[l]:
                    ada(l, n)
                pe.wait_ge(prob_ready, TT * l + 1)
                pe.wait_ge(yc_ready, TT * l + 1)
                for h in range(HEADS):
                    m = pe.transpose(ps[:, 0, h * P:(h + 1) * P], p0[:, h, :], ident[:, :])
                m.then_inc(pt_mm, 1)
                pe.wait_ge(prob_ready, TT * l + 2)
                pe.wait_ge(yc_ready, TT * l + 2)
                for bank, s in ((1, 0), (3, 1)):
                    for h in range(HEADS):
                        m = pe.transpose(ps[:, bank, h * P:(h + 1) * P], p1[:, h, s * P:(s + 1) * P], ident[:, :])
                    m.then_inc(pt_mm, 1)
                pe.wait_ge(pt_ready, 3 * (l + 1))
                for h in range(HEADS):
                    bank, o = 2 + 2 * (h // 2), (h % 2) * T
                    pe.matmul(ps[:, bank, o:o + T], v_sb[:, 0, h * VH:(h + 1) * VH], p_t0[:, h, :], start=True, stop=False)
                    m = pe.matmul(ps[:, bank, o + P:o + T], v_sb[:, 1, h * VH:(h + 1) * VH], p_t1[:, h, :], start=False, stop=True)
                m.then_inc(attn_mm, 1)
                pe.wait_ge(attn_sq, l + 1)
                use_bank7(("ssq_attn", l))
                for t in range(TT):
                    for c in range(HEADS):
                        m = pe.matmul(ps[:, 7, t:t + 1], sq[:, c, t * P:(t + 1) * P], ones[:, 0:1],
                                      start=(c == 0), stop=(c == HEADS - 1))
                m.then_inc(bank7_full, 1)
                pe.wait_ge(attn_scaled, l + 1)
                wait_load(pe, ("oa", l))
                oa = slot_of(("oa", l)).rearrange("p (c n) -> p c n", c=4)
                for t in range(TT):
                    for half in range(2):
                        for c in range(4):
                            m = pe.matmul(ps[:, (0, 5)[t] + half, :], a_t[:, c, t * P:(t + 1) * P],
                                          oa[:, c, half * 512:(half + 1) * 512], start=(c == 0), stop=(c == 3))
                    m.then_inc(ya_mm, 1)

            def three(o, x_hi, x_lo, hi, lo, first, last):
                pe.matmul(o, x_lo, hi, start=first, stop=False, skip_group_check=True)
                pe.matmul(o, x_hi, lo, start=False, stop=False, skip_group_check=True)
                return pe.matmul(o, x_hi, hi, start=False, stop=last, skip_group_check=True)

            mixer(0)
            turn_input(1)
            pe.wait_ge(h_lo_ready, 1)

            def ff_rows(s, what, bank):
                for k in range(2):
                    u = ff_first_unit(s) + 2 * what + k
                    pe.wait_ge(unit_lo, u + 1)
                    hi = w_hi[:, u % SRING, :].rearrange("p (c n) -> p c n", c=4)
                    lo = w_lo[:, u % SRING, :].rearrange("p (c n) -> p c n", c=4)
                    for t in range(TT):
                        for c in range(4):
                            cc, tok = 4 * k + c, slice(t * P, (t + 1) * P)
                            m = three(ps[:, bank, t * 256:(t + 1) * 256], h_hi[:, cc, tok], h_lo[:, cc, tok],
                                      hi[:, c, :], lo[:, c, :], k == 0 and t == 0 and c == 0,
                                      k == 1 and t == TT - 1 and c == 3)
                    m.then_inc(unit_used, 1)

            def ff_turn(s):
                pe.wait_ge(hid_done, s + 1)
                if s >= 1:
                    pe.wait_ge(hidt_lo, s)
                for f in range(2):
                    for t in range(TT):
                        m = pe.transpose(ps[:, 2, f * T + t * P:f * T + (t + 1) * P],
                                         hid[:, 2 * t + f, :], ident[:, :])
                m.then_inc(hidt_mm, 1)

            def ff_down(s):
                pe.wait_ge(hidt_lo, s + 1)
                for f in range(2):
                    u = (ff_first_unit(s + 1) + 4 if s < FF_STEPS - 1 else FF_UNITS - 2) + f
                    pe.wait_ge(unit_lo, u + 1)
                    for t in range(TT):
                        x = slice(f * T + t * P, f * T + (t + 1) * P)
                        for half in range(2):
                            cols = slice(half * 512, (half + 1) * 512)
                            m = three(ps[:, 3 + 2 * t + half, :], hid_hi[:, x], hid_lo[:, x], w_hi[:, u % SRING, cols],
                                      w_lo[:, u % SRING, cols], s == 0 and f == 0, s == FF_STEPS - 1 and f == 1)
                    m.then_inc(unit_used, 1)

            for s in range(FF_STEPS + 1):
                if s < FF_STEPS:
                    if s >= 1:
                        pe.wait_ge(silu_done, s)
                    ff_rows(s, 0, 0)
                    if s >= 1:
                        ff_turn(s - 1)
                        for strip in FF_ADA[s - 1]:
                            ada(*strip[1:])
                    ff_rows(s, 1, 1)
                else:
                    ff_turn(s - 1)
                    for strip in FF_ADA[s - 1]:
                        ada(*strip[1:])
                if s >= 1:
                    ff_down(s - 1)

            mixer(1)
            turn_input(3)
            pe.wait_ge(ht_ready, 4 * KC)
            pe.wait_ge(rt_loaded, 32)
            for t in range(TT):
                o = ps[:, 4, t * E:(t + 1) * E]
                for c in range(KC):
                    pe.matmul(o, h_t[:, c, t * P:(t + 1) * P], router_w[:, c, :], start=(c == 0), stop=False)
                m = pe.matmul(o, ones[0:1, :], router_b[:, :], start=False, stop=True)
            m.then_inc(logit_mm, 1)
            pe.wait_ge(chosen_ready, 1)
            pe.matmul(ps[:, 4, 64:64 + E], before[:, :], chosen[:, 0, :], start=True, stop=True)
            pe.matmul(ps[:, 4, 64 + E:64 + 2 * E], before[:, :], chosen[:, 1, :], start=True, stop=False)
            pe.matmul(ps[:, 4, 64 + E:64 + 2 * E], ones[:, :], chosen[:, 0, :], start=False, stop=True)
            pe.matmul(ps[:, 4, 64 + 2 * E:64 + 3 * E], ones[:, :], chosen[:, 0, :], start=True, stop=False)
            pe.matmul(ps[:, 4, 64 + 2 * E:64 + 3 * E], ones[:, :], chosen[:, 1, :], start=False, stop=True).then_inc(place_mm, 1)

            def gather(i):
                pe.wait_ge(sel_ready, i + 1)
                for c in range(KC):
                    for t in range(TT):
                        m = pe.matmul(ps[:, 5 + c // 4, (c % 4) * P:(c % 4 + 1) * P], x_sb[:, t, c * P:(c + 1) * P],
                                      sel[:, t, :], start=(t == 0), stop=(t == TT - 1))
                m.then_inc(xg_mm, 1)

            pe.wait_ge(bank7_free, len(BANK7))
            gather(0)

            def item(i):
                units, steps = i * E_UNITS, i * E_STEPS

                def unit(k):
                    pe.wait_ge(unit_lo, units + (FF_UNITS + k + 1))
                    return (FF_UNITS + k) % SRING

                def rows(j, what, bank):
                    for k in range(4):
                        q = unit(moe_first_unit(j) + 4 * what + k)
                        for c in range(2):
                            cols = slice(c * 512, (c + 1) * 512)
                            cc = 2 * k + c
                            m = three(ps[:, bank, :], xg_hi[:, cc, :], xg_lo[:, cc, :], w_hi[:, q, cols], w_lo[:, q, cols],
                                      cc == 0, cc == KC - 1)
                        m.then_inc(unit_used, 1)

                def turn(j):
                    pe.wait_ge(hid_done, steps + (FF_STEPS + j + 1))
                    pe.wait_ge(hidt_lo, steps + (FF_STEPS + j))
                    for f in range(4):
                        m = pe.transpose(ps[:, 2, f * P:(f + 1) * P], hid[:, f, :], ident[:, :])
                    m.then_inc(hidt_mm, 1)

                def down(j):
                    pe.wait_ge(hidt_lo, steps + (FF_STEPS + j + 1))
                    for f in range(4):
                        q = unit((moe_first_unit(j + 1) + 8 if j < E_STEPS - 1 else E_UNITS - 4) + f)
                        for half in range(2):
                            cols = slice(half * 512, (half + 1) * 512)
                            m = three(ps[:, 3 + half, :], hid_hi[:, f * P:(f + 1) * P], hid_lo[:, f * P:(f + 1) * P],
                                      w_hi[:, q, cols], w_lo[:, q, cols], j == 0 and f == 0, j == E_STEPS - 1 and f == 3)
                        m.then_inc(unit_used, 1)

                pe.wait_ge(xg_lo_ready, i + 1)
                for j in range(E_STEPS):
                    if j == 1:
                        pe.wait_ge(acc_ready, i * 4 + 1)
                    else:
                        pe.wait_ge(silu_done, steps + (FF_STEPS + max(j - 1, 0)))
                    rows(j, 0, GATE_BANKS[j % 2])
                    if j == 1:
                        for t in range(TT):
                            m = pe.transpose(ps[:, 5, t * P:(t + 1) * P], sel[:, t, :], ident[:, :])
                        m.then_inc(selt_mm, 1)
                    if j >= 1:
                        turn(j - 1)
                    rows(j, 1, 1)
                    if j >= 1:
                        down(j - 1)
                turn(E_STEPS - 1)
                pe.wait_ge(selt_ready, i + 1)
                gather(i + 1)
                down(E_STEPS - 1)
                pe.wait_ge(xg_ready, i + 2)
                pe.wait_ge(xg2_ready, i + 2)
                for half in range(2):
                    pe.wait_ge((y_ready, y2_ready)[half], i + 1)
                    for t in range(TT):
                        pe.matmul(ps[:, SCATTER_BANKS[t][half], :], sel_t[:, t, :], y_sb[:, half * 512:(half + 1) * 512],
                                  start=True, stop=True).then_inc(scatter_mm, 1)

            with pe.Fori(0, E) as i:
                item(i)
            n_items = pe.value_load(plan_i[0:1, 0:1], min_val=E, max_val=ITEMS)
            for r in range(OVER):
                with pe.If(n_items > E + r):
                    item(E + r)


_INS = ['x', 'c', 'positions', 'w_in', 'q_norm_g', 'kv_norm_g', 'w_uq', 'w_ukv', 'conv_w', 'mix_norm_g', 'w_o',
        'w_ada', 'b_ada', 'ln1_g', 'ln1_b', 'ln2_g', 'ln2_b', 'ffn_w_gate', 'ffn_w_up', 'ffn_w_down',
        'moe_router_w', 'moe_router_b', 'moe_w_gate', 'moe_w_up', 'moe_w_down']


def kernel(**inputs):
    import numpy as _np
    import concourse.bacc as _bacc
    from concourse import mybir as _mybir
    from concourse.bass_utils import run_bass_kernel_spmd as _run

    nc = _bacc.Bacc("TRN2", target_bir_lowering=False, num_devices=1, dynamic_dma_scratch_size=1024)
    arrays, args = {}, {}
    for name in _INS:
        v = _np.ascontiguousarray(inputs[name])
        arrays[f"in_{name}_dram"] = v
        args[name] = nc.dram_tensor(f"in_{name}_dram", v.shape, _mybir.dt.from_np(v.dtype), kind="ExternalInput").ap()
    out = nc.dram_tensor("out_0_dram", (1, T, D), _mybir.dt.float32, kind="ExternalOutput").ap()
    trunk(nc, args, out)
    r = _run(nc, [arrays], core_ids=[0])
    return r.results[0]["out_0_dram"]
```

```python
from contextlib import ExitStack

import numpy as np

import concourse.bass as bass
from concourse import mybir

F32 = mybir.dt.float32
F32R = mybir.dt.float32r
I32 = mybir.dt.int32
ALU = mybir.AluOpType
ACT = mybir.ActivationFunctionType
AX_X = mybir.AxisListType.X

P = 128
D = 1024
KC = D // P
T = 256
TT = T // P
L = 2
HEADS, NOPE, ROPE, VH = 4, 128, 64, 128
HALF = ROPE // 2
Q_LORA, KV_LORA = 256, 128
ZA = Q_LORA + KV_LORA + ROPE
D_CONV = 512
CC = D_CONV // P
FF = 2816
FF_STEPS = FF // 256
E = 8
FE = 3584
E_STEPS = FE // 512
OVER = 3
ITEMS = E + OVER
SCALE = float(NOPE + ROPE) ** -0.5
ALPHA = float((2 * L) ** 0.25)
RMS_EPS, LN_EPS = 1e-6, 1e-5
MASKED = -1e30
ROPE_BASE = 10000.0
TWO_PI = 2.0 * np.pi

RING = 7
SLOT = 4096
UNIT = 1024
SRING = 4
HEAD = 4
SCATTER_BANKS = ((5, 6), (7, 2))
GATE_BANKS = (0, 7)
FF_UNITS = 6 * FF_STEPS
E_UNITS = 12 * E_STEPS
E_LOADS = 3 * E_STEPS

SMALL = (("q_norm_g", Q_LORA // P), ("kv_norm_g", KV_LORA // P), ("mix_norm_g", KC), ("conv_w", 3 * CC),
         ("ln1_g", KC), ("ln1_b", KC), ("ln2_g", KC), ("ln2_b", KC))
PRM_AT = {name: KC + L * sum(rows for _, rows in SMALL[:n]) for n, (name, _) in enumerate(SMALL)}
PRM = KC + L * sum(rows for _, rows in SMALL)
PRM_LOADS = 1 + len(SMALL) + 1 + 1
STRIPS = 6 * D // 512

BANK7 = ["params"] + [("ada", 0, n) for n in range(4)]
BANK7 += [("ada", 0, n) for n in range(4, 9)] + [("ssq_conv", 0), ("ada", 0, 9), ("ssq_attn", 0)]
BANK7 += [("ada", 0, 10), ("ada", 0, 11)] + [("ada", 1, n) for n in range(11)]
BANK7 += [("ssq_conv", 1), ("ada", 1, 11), ("ssq_attn", 1)]
ADA_ORDER = [u for u in BANK7 if u[0] == "ada"]

FF_ADA = [("ada", 0, 10), ("ada", 0, 11)] + [("ada", 1, n) for n in range(FF_STEPS - 2)]
EARLY = 4
MIX_ADA = (((5, 6), (7, 8), (9,)), ((), (9, 10), (11,)))


def split2pi():
    parts, rest = [], TWO_PI
    for bits in (8, 9, 9):
        scale = 2.0 ** (bits - 1 - np.floor(np.log2(abs(rest))))
        part = float(np.floor(rest * scale) / scale)
        parts.append(part)
        rest -= part
    parts.append(float(np.float32(rest)))
    return parts


def ff_first_unit(s):
    return 0 if s == 0 else 4 + 6 * (s - 1)


def moe_first_unit(j):
    return 0 if j == 0 else 8 + 12 * (j - 1)


def trunk(nc, a, out):
    with ExitStack() as ctx:
        def sb(name, shape, dt=F32, stack=ctx):
            return stack.enter_context(nc.sbuf_tensor(name, shape, dt))

        sems = {}

        def sem(name):
            sems[name] = ctx.enter_context(nc.semaphore(name))
            return sems[name]

        ps = ctx.enter_context(nc.psum_tensor("ps", [P, 8, 512], F32))

        raw = sb("raw", [P, RING, SLOT])
        x_sb = sb("x_sb", [P, TT, D])
        yv = sb("yv", [P, TT, D])
        h_t = sb("h_t", [P, KC, T])
        ln_g = sb("ln_g", [P, D])
        ln_b = sb("ln_b", [P, D])
        gate1 = sb("gate1", [P, D])
        gate2 = sb("gate2", [P, D])
        ada_acc = sb("ada_acc", [P, 2, 512])
        ada_bias = sb("ada_bias", [STRIPS, L, 512])
        ident = sb("ident", [P, P])
        ones = sb("ones", [P, P])
        causal = sb("causal", [P, P])
        before = sb("before", [P, P])
        slot_no = sb("slot_no", [P, P])
        slot_i = sb("slot_i", [P, P], I32)
        prm_rows = sb("prm_rows", [PRM, P])
        prm = sb("prm", [P, PRM])
        c_act = sb("c_act", [P, KC])
        modc = sb("modc", [P, L, 4, KC])
        modf = sb("modf", [P, 2 * L, 2, KC])
        pos_i = sb("pos_i", [P, TT], I32)
        pos_f = sb("pos_f", [P, TT])
        freq = sb("freq", [P, HALF])
        trig = sb("trig", [P, 2, TT, HALF])
        ang = sb("ang", [P, 2, TT, HALF])
        turns = sb("turns", [P, 2, TT, HALF])
        eps = sb("eps", [P, 3])
        stats = sb("stats", [P, TT, 2, 6])
        meanvar = sb("meanvar", [P, TT, 2])
        std = sb("std", [P, TT])
        rstd = sb("rstd", [P, TT])
        ssq = sb("ssq", [P, 2, TT])
        rms = sb("rms", [P, 2, TT])
        rrms = sb("rrms", [P, 2, TT])
        gstd = sb("gstd", [P, 2, TT])
        grr = sb("grr", [P, 2, TT])
        mx = sb("mx", [P, TT, HEADS])
        nmx = sb("nmx", [P, TT, HEADS])
        den = sb("den", [P, TT, HEADS])
        rden = sb("rden", [P, TT, HEADS])
        router_w = sb("router_w", [P, KC, E])
        router_b = sb("router_b", [1, E])
        logit = sb("logit", [P, TT, E])
        top = sb("top", [P, TT, 8])
        above = sb("above", [P, TT, E])
        pads = sb("pads", [P, 3, TT, 2 * E])
        n_above = sb("n_above", [P, TT])
        chosen = sb("chosen", [P, TT, E])
        expo = sb("expo", [P, TT, E])
        exsum = sb("exsum", [P, TT])
        exinv = sb("exinv", [P, TT])
        place = sb("place", [P, TT, ITEMS + 1])
        share = sb("share", [P, TT, ITEMS + 1])
        cnt = sb("cnt", [P, 3, 2 * E])
        rank = sb("rank", [P, E])
        e_no = sb("e_no", [P, E])
        pick = sb("pick", [P, OVER, E])
        picked = sb("picked", [P, OVER, 5, E])
        plan_f = sb("plan_f", [P, 1 + OVER])
        plan_i = sb("plan_i", [P, 1 + OVER], I32)

        mix = ExitStack()
        zn = sb("zn", [P, TT, Q_LORA + KV_LORA], stack=mix)
        kr = sb("kr", [P, TT, 2, 2, ROPE], stack=mix)
        cq_t = sb("cq_t", [P, 2, T], stack=mix)
        ckv_t = sb("ckv_t", [P, T], stack=mix)
        kr_t = sb("kr_t", [P, 2, T], stack=mix)
        qr = sb("qr", [P, TT, HEADS, ROPE], stack=mix)
        qr_t = sb("qr_t", [P, 2, T], stack=mix)
        qn_t = sb("qn_t", [P, HEADS, T], stack=mix)
        kn_t = sb("kn_t", [P, HEADS, T], stack=mix)
        v_sb = sb("v_sb", [P, TT, HEADS * VH], stack=mix)
        gb_t = sb("gb_t", [P, CC, T], stack=mix)
        gc_t = sb("gc_t", [P, CC, T], stack=mix)
        cu = sb("cu", [P, CC, T + 2], stack=mix)
        cv = sb("cv", [P, CC, T], stack=mix)
        mix.close()
        rp_k = cv[:, 0, :].rearrange("p (k t r) -> p k t r", k=4, t=TT)
        rp_q = cv[:, :, :].rearrange("p k (t h r) -> p k t h r", t=TT, h=HEADS)
        p0 = zn[:, :, :].rearrange("p t n -> p (t n)")[:, 0:HEADS * P].rearrange("p (h s) -> p h s", h=HEADS)
        p1, cv_t, a_t = gb_t, gc_t, cv
        p_t0, p_t1 = qn_t, kn_t[:, :, 0:P]
        sq = h_t[:, 0:CC, :]
        att_tmp = (v_sb[:, :, :].rearrange("p t n -> p (t n)"), gb_t[:, :, :].rearrange("p c t -> p (c t)"))
        ff = ExitStack()
        w_hi = sb("w_hi", [P, SRING, UNIT], F32R, ff)
        w_lo = sb("w_lo", [P, SRING, UNIT], F32R, ff)
        h_hi = sb("h_hi", [P, KC, T], F32R, ff)
        h_lo = sb("h_lo", [P, KC, T], F32R, ff)
        sil = sb("sil", [P, 512], stack=ff)
        hid_hi = sb("hid_hi", [P, 512], F32R, ff)
        hid_lo = sb("hid_lo", [P, 512], F32R, ff)
        hid = h_t[:, 4:8, P:T]
        sel = h_t[:, 0:2, P:T]
        sel_t = h_lo[:, 0:2, P:T]
        y_hi = (h_hi[:, 0:4, P:T], h_hi[:, 4:8, P:T])
        y_lo = (hid_hi, hid_lo)
        ff.close()
        moe_acc = yv
        xg_hi, xg_lo, xg = h_hi[:, :, 0:P], h_lo[:, :, 0:P], h_t[:, :, 0:P]

        slot_full = [sem(f"slot_full{k}") for k in range(RING)]
        half_full = [sem(f"half_full{k}") for k in range(EARLY)]
        ada_summed = sem("ada_summed")
        unit_hi, unit_lo, unit_used = sem("unit_hi"), sem("unit_lo"), sem("unit_used")
        prm_loaded, x_loaded, ln_loaded, rt_loaded = (sem("prm_loaded"), sem("x_loaded"), sem("ln_loaded"),
                                                      sem("rt_loaded"))
        const_order, consts = sem("const_order"), sem("consts")
        dve_order, act_order = sem("dve_order"), sem("act_order")
        bank7_full, bank7_free = sem("bank7_full"), sem("bank7_free")
        c_ready, angles, trig_ready = sem("c_ready"), sem("angles"), sem("trig_ready")
        xn_ready, gained, fold_ready = sem("xn_ready"), sem("gained"), sem("fold_ready")
        x_ready, xt_mm, ht_ready = sem("x_ready"), sem("xt_mm"), sem("ht_ready")
        ht2_ready, h_hi_ready, h_lo_ready = sem("ht2_ready"), sem("h_hi_ready"), sem("h_lo_ready")
        za_mm, zb_mm, zc_mm, zu_mm = sem("za_mm"), sem("zb_mm"), sem("zc_mm"), sem("zu_mm")
        gb_ready, gc_ready, cu_ready = sem("gb_ready"), sem("gc_ready"), sem("cu_ready")
        ssq_ready, rms_ready, zn_ready = sem("ssq_ready"), sem("rms_ready"), sem("zn_ready")
        znt_mm, znt_ready = sem("znt_mm"), sem("znt_ready")
        qn_mm, kn_mm, qr_mm, v_mm = sem("qn_mm"), sem("kn_mm"), sem("qr_mm"), sem("v_mm")
        qn_ready, kn_ready, qr_ready, v_ready = (sem("qn_ready"), sem("kn_ready"), sem("qr_ready"),
                                                 sem("v_ready"))
        qrt_mm, qrt_ready = sem("qrt_mm"), sem("qrt_ready")
        score_mm, max_ready, exp_ready, prob_ready = (sem("score_mm"), sem("max_ready"), sem("exp_ready"),
                                                      sem("prob_ready"))
        pt_mm, pt_ready = sem("pt_mm"), sem("pt_ready")
        conv_ready, conv_sq, conv_scaled = sem("conv_ready"), sem("conv_sq"), sem("conv_scaled")
        gstd_ready, grr_ready = sem("gstd_ready"), sem("grr_ready")
        yc_mm, yc_ready = sem("yc_mm"), sem("yc_ready")
        attn_mm, attn_sq, attn_scaled, ya_mm = sem("attn_mm"), sem("attn_sq"), sem("attn_scaled"), sem("ya_mm")
        var_ready, std_ready = sem("var_ready"), sem("std_ready")
        silu_done, hid_done = sem("silu_done"), sem("hid_done")
        hidt_mm, hid_hi_ready, hid_lo_ready = sem("hidt_mm"), sem("hid_hi_ready"), sem("hid_lo_ready")
        logit_mm, rel_ready, expo_ready, chosen_ready = (sem("logit_mm"), sem("rel_ready"), sem("expo_ready"),
                                                         sem("chosen_ready"))
        place_mm, plan_ready = sem("place_mm"), sem("plan_ready")
        sel_ready, selt_mm, selt_ready = sem("sel_ready"), sem("selt_mm"), sem("selt_ready")
        xg_mm, xg_ready, xg_hi_ready, xg_lo_ready = (sem("xg_mm"), sem("xg_ready"), sem("xg_hi_ready"),
                                                     sem("xg_lo_ready"))
        y_ready, y_lo_ready, scatter_mm, acc_ready = (sem("y_ready"), sem("y_lo_ready"), sem("scatter_mm"),
                                                      sem("acc_ready"))
        xg2_ready, xg2_hi = sem("xg2_ready"), sem("xg2_hi")
        out_done = sem("out_done")

        def strip_src(l, n):
            return a["w_ada"][l][:, n * 512:(n + 1) * 512].rearrange("(c p) n -> p c n", p=P)

        def win_src(l, lo, hi):
            return a["w_in"][l][:, lo:hi].rearrange("(c p) n -> p c n", p=P)

        loads = []

        def load_ada(l, n):
            k = ADA_ORDER.index(("ada", l, n))
            src, parts = strip_src(l, n), 2 if k < EARLY else 1
            loads.append((("ada", l, n), [(q * SLOT // parts, (q + 1) * SLOT // parts, KC // parts,
                                           src[:, q * KC // parts:(q + 1) * KC // parts, :]) for q in range(parts)],
                          (ada_summed, k + 1)))

        def load_pe(name, parts, released):
            loads.append((name, parts, released))

        for n in range(4):
            load_ada(0, n)
        for l in range(L):
            z0 = ZA
            load_pe(("wa", l), [(0, KC * ZA, KC, win_src(l, 0, ZA))], (za_mm, TT * (l + 1)))
            load_pe(("wb", l), [(0, SLOT, KC, win_src(l, z0, z0 + D_CONV))], (zb_mm, l + 1))
            load_pe(("wc", l), [(0, SLOT, KC, win_src(l, z0 + D_CONV, z0 + 2 * D_CONV))], (zc_mm, l + 1))
            for n in ((4,) if l == 0 else ()) + MIX_ADA[l][0]:
                load_ada(l, n)
            load_pe(("wu", l), [(0, SLOT, KC, win_src(l, z0 + 2 * D_CONV, z0 + 3 * D_CONV))], (zu_mm, l + 1))
            for n in MIX_ADA[l][1]:
                load_ada(l, n)
            load_pe(("qkv", l), [(0, 2 * 768, 2, a["w_uq"][l].rearrange("(c p) n -> p c n", p=P)),
                                 (2 * 768, 2 * 768 + 1024, 1, a["w_ukv"][l].rearrange("(c p) n -> p c n", p=P))], (v_mm, l + 1))
            for n in MIX_ADA[l][2]:
                load_ada(l, n)
            load_pe(("oc", l), [(0, SLOT, 4, a["w_o"][l][512:1024, :].rearrange("(c p) n -> p c n", p=P))],
                    (yc_mm, TT * (l + 1)))
            load_pe(("oa", l), [(0, SLOT, 4, a["w_o"][l][0:512, :].rearrange("(c p) n -> p c n", p=P))],
                    (ya_mm, TT * (l + 1)))
            if l == 0:
                for s in range(FF_STEPS + 1):
                    if s < FF_STEPS:
                        cols = slice(s * 256, (s + 1) * 256)
                        loads.append((("gu", s), [
                            (0, 2048, KC, a["ffn_w_gate"][0][:, cols].rearrange("(c p) n -> p c n", p=P)),
                            (2048, 4096, KC, a["ffn_w_up"][0][:, cols].rearrange("(c p) n -> p c n", p=P))],
                            (unit_lo, ff_first_unit(s) + 4)))
                    if s < FF_STEPS:
                        load_ada(*FF_ADA[s][1:])
                    if s >= 1:
                        rows = slice((s - 1) * 256, s * 256)
                        end = ff_first_unit(s) + 6 if s < FF_STEPS else FF_UNITS
                        loads.append((("dn", s - 1), [
                            (0, 2048, 2, a["ffn_w_down"][0][rows, :].rearrange("(c p) n -> p c n", p=P))],
                            (unit_lo, end)))

        place_of, full_at = {}, {}
        filled = [0] * RING
        for n, (name, parts, _) in enumerate(loads):
            filled[n % RING] += 16 * (1 if n < EARLY else len(parts))
            place_of[name] = n % RING
            full_at[name] = filled[n % RING]
        L0 = len(loads)

        def slot_of(name):
            return raw[:, place_of[name], :]

        def wait_load(eng, name):
            eng.wait_ge(slot_full[place_of[name]], full_at[name])

        def moe_slot(m):
            return (L0 + m) % RING

        def moe_full(i, m):
            k = moe_slot(m)
            nth = sum(1 for q in range(m) if moe_slot(q) == k) + 1
            return i * (16 * (E_LOADS // RING)) + (filled[k] + 16 * nth)

        e_loads = []
        for j in range(E_STEPS + 1):
            if j < E_STEPS:
                e_loads += [("g", j), ("u", j)]
            if j >= 1:
                e_loads.append(("d", j - 1))

        def bank7(use):
            return BANK7.index(use)

        def prm_col(l, name, k=0, n=1):
            base = PRM_AT[name] + l * dict(SMALL)[name] + k
            return prm[:, base:base + n]

        block = ctx.enter_context(nc.Block())

        @block.sync
        def _(sp):
            sp.dma_start(prm_rows[0:KC, :], a["c"].rearrange("a (k p) -> (a k) p", p=P)).then_inc(prm_loaded, 16)
            for name, rows in SMALL:
                src = a[name].rearrange("l j (k p) -> (l j k) p" if name == "conv_w" else "l (k p) -> (l k) p", p=P)
                sp.dma_start(prm_rows[PRM_AT[name]:PRM_AT[name] + L * rows, :], src).then_inc(prm_loaded, 16)
            sp.dma_start(ada_bias[:, :, :], a["b_ada"].rearrange("l (k n) -> k l n", n=512)).then_inc(prm_loaded, 16)
            sp.dma_start(pos_i[:, :], a["positions"][0].rearrange("(t p) -> p t", p=P),
                          allow_slow_non_contiguous=True).then_inc(prm_loaded, 16)
            for n, (name, parts, _) in enumerate(loads):
                if n >= RING:
                    s, value = loads[n - RING][2]
                    sp.wait_ge(s, value)
                for lo, hi, chunks, src in parts:
                    dst = raw[:, n % RING, lo:hi].rearrange("p (c n) -> p c n", c=chunks)
                    sp.dma_start(dst, src).then_inc(half_full[n] if n < EARLY and lo == 0 else slot_full[n % RING], 16)
                if name == ("ada", 0, 3):
                    for t in range(TT):
                        sp.dma_start(x_sb[:, t, :], a["x"][0, t * P:(t + 1) * P, :]).then_inc(x_loaded, 16)

            def expert_loads(i, e, first):
                for m, (kind, j) in enumerate(e_loads):
                    if first and m < RING:
                        s, value = loads[L0 + m - RING][2]
                        sp.wait_ge(s, value)
                    else:
                        sp.wait_ge(unit_lo, i * E_UNITS + (FF_UNITS + 4 * (m - RING + 1)))
                    if kind == "d":
                        src = a["moe_w_down"][0][bass.ds(e, 1), j * 512:(j + 1) * 512, :]
                        src = src.rearrange("a (c p) n -> p (a c) n", p=P)
                    else:
                        w = a["moe_w_gate"] if kind == "g" else a["moe_w_up"]
                        src = w[0][bass.ds(e, 1), :, j * 512:(j + 1) * 512].rearrange("a (c p) n -> p (a c) n", p=P)
                    k = moe_slot(m)
                    dst = raw[:, k, :].rearrange("p (c n) -> p c n", c=4 if kind == "d" else KC)
                    sp.dma_start(dst, src).then_inc(slot_full[k], 16)

            expert_loads(0, 0, True)
            with sp.Fori(1, E) as e:
                expert_loads(e, e, False)
            sp.wait_ge(plan_ready, 1)
            n_items = sp.value_load(plan_i[0:1, 0:1], min_val=E, max_val=ITEMS)
            for r in range(OVER):
                with sp.If(n_items > E + r):
                    e = sp.value_load(plan_i[0:1, 1 + r:2 + r], min_val=0, max_val=E - 1)
                    expert_loads(E + r, e, False)
            for t in range(TT):
                sp.wait_ge(x_ready, TT * (2 * L - 1) + t + 1)
                sp.dma_start(out[0, t * P:(t + 1) * P, :], x_sb[:, t, :]).then_inc(out_done, 16)
            sp.wait_ge(out_done, 16 * TT)

        @block.gpsimd
        def _(pool):
            pool.memset(ident[:, :], 0.0).then_inc(const_order, 1)
            pool.memset(causal[:, :], 0.0).then_inc(const_order, 1)
            pool.memset(before[:, :], 1.0).then_inc(const_order, 1)
            pool.memset(ones[:, :], 1.0)
            for k in range(HALF):
                pool.memset(freq[:, k:k + 1], float(np.float32(ROPE_BASE) ** np.float32(-2.0 * k / ROPE)))
            pool.memset(eps[:, 0:1], RMS_EPS)
            pool.memset(eps[:, 1:2], LN_EPS)
            pool.memset(eps[:, 2:3], 0.0)
            pool.iota(slot_i[:, :], [[1, P]], base=0, channel_multiplier=0)
            pool.wait_ge(const_order, 3)
            pool.affine_select(out=ident[:, :], in_=ident[:, :], compare_op=ALU.not_equal, fill=1.0,
                               base=0, pattern=[[-1, P]], channel_multiplier=1)
            pool.affine_select(out=causal[:, :], in_=causal[:, :], compare_op=ALU.is_ge, fill=MASKED,
                               base=0, pattern=[[-1, P]], channel_multiplier=1)
            pool.affine_select(out=before[:, :], in_=before[:, :], compare_op=ALU.is_gt, fill=0.0,
                               base=0, pattern=[[1, P]], channel_multiplier=-1).then_inc(consts, 1)
            for k in range(2 * L - 1):
                pool.wait_ge(ln_loaded, 32 * (k + 1))
                for t in range(TT):
                    pool.wait_ge(xn_ready, TT * k + t + 1)
                    pool.tensor_tensor(x_sb[:, t, :], yv[:, t, :], ln_g[:, :], ALU.mult).then_inc(gained, 1)
                for t in range(TT):
                    pool.wait_ge(gained, TT * k + t + 1)
                    pool.tensor_tensor(x_sb[:, t, :], x_sb[:, t, :], ln_b[:, :], ALU.add).then_inc(x_ready, 1)

        @block.scalar
        def _(act):
            count = [0]

            def link(ins):
                count[0] += 1
                ins.then_inc(act_order, 1)
                act.wait_ge(act_order, count[0])

            def drain_ada(l, n):
                use = bank7(("ada", l, n))
                act.wait_ge(bank7_full, use + 1)
                vec, half = n // 2, n % 2
                if vec in (2, 5):
                    act.activation((gate1 if vec == 2 else gate2)[:, half * 512:(half + 1) * 512], ps[:, 7, :], ACT.Copy).then_inc(bank7_free, 1)
                else:
                    row = {0: 0, 1: 1, 3: 2, 4: 3}[vec]
                    one = vec in (1, 4)
                    act.activation(modc[:, l, row, 4 * half:4 * half + 4], ps[:, 7, 0:4], ACT.Identity,
                                   bias=ones[:, 0:1] if one else eps[:, 2:3]).then_inc(bank7_free, 1)

            def modulate(v, l, row, last):
                if v == 0:
                    act.wait_ge(bank7_free, bank7(last) + 1)
                    shift, scale = modc[:, l, row, :], modc[:, l, row + 1, :]
                else:
                    act.wait_ge(fold_ready, v)
                    shift, scale = modf[:, v, 0, :], modf[:, v, 1, :]
                for n, c0 in enumerate((0, 4)):
                    act.wait_ge(xt_mm, KC * v + c0 + 2)
                    for c in (c0, c0 + 1):
                        act.activation(h_t[:, c, :], ps[:, c // 2, (c % 2) * T:(c % 2) * T + T], ACT.Identity,
                                       scale=scale[:, c:c + 1], bias=shift[:, c:c + 1]).then_inc(ht_ready, 1)
                    if v == 1:
                        act.wait_ge(ht_ready, KC // 2 * v + 2 * n + 2)
                        act.activation(h_hi[:, c0:c0 + 2, :], h_t[:, c0:c0 + 2, :], ACT.Copy).then_inc(h_hi_ready, 1)

            def layer_std(k):
                for t in range(TT):
                    act.wait_ge(var_ready, TT * k + t + 1)
                    act.activation(std[:, t:t + 1], meanvar[:, t, 1:2], ACT.Sqrt, bias=eps[:, 1:2]).then_inc(std_ready, 1)

            act.dma_start(router_w[:, :, :], a["moe_router_w"][0].rearrange("(c p) e -> p c e", p=P)).then_inc(rt_loaded, 16)
            act.dma_start(router_b[:, :], a["moe_router_b"]).then_inc(rt_loaded, 16)

            def ln_rows(k):
                if k >= 1:
                    act.wait_ge(x_ready, TT * k)
                for dst, src in ((ln_g, a[f"ln{k % 2 + 1}_g"]), (ln_b, a[f"ln{k % 2 + 1}_b"])):
                    act.dma_start(dst[:, :], src[k // 2:k // 2 + 1, :].to_broadcast([P, D])).then_inc(ln_loaded, 16)

            act.wait_ge(consts, 1)
            act.wait_ge(bank7_full, 1)
            link(act.activation(prm[:, :], ps[:, 7, 0:PRM], ACT.Copy))
            act.activation(c_act[:, :], prm[:, 0:KC], ACT.Silu).then_inc(bank7_free, 1)
            act.wait_ge(angles, 1)
            act.activation(trig[:, :, :, :], ang[:, :, :, :], ACT.Sin).then_inc(trig_ready, 1)
            for n in range(4):
                drain_ada(0, n)

            def mixer(l):
                modulate(2 * l, l, 0, ("ada", l, 3))
                for t in range(TT):
                    act.wait_ge(za_mm, TT * l + t + 1)
                    act.activation(v_sb[:, t, 0:Q_LORA], ps[:, 4 + t, 0:Q_LORA], ACT.Square,
                                   accum_out=ssq[:, 0, t:t + 1])
                    act.activation(v_sb[:, t, Q_LORA:Q_LORA + KV_LORA], ps[:, 4 + t, Q_LORA:Q_LORA + KV_LORA], ACT.Square,
                                   accum_out=ssq[:, 1, t:t + 1]).then_inc(ssq_ready, 1)
                act.wait_ge(ssq_ready, TT * (l + 1))
                act.activation(rms[:, 0, :], ssq[:, 0, :], ACT.Sqrt, scale=1.0 / Q_LORA, bias=eps[:, 0:1])
                act.activation(rms[:, 1, :], ssq[:, 1, :], ACT.Sqrt, scale=1.0 / KV_LORA, bias=eps[:, 0:1]).then_inc(rms_ready, 1)
                act.wait_ge(zb_mm, l + 1)
                act.activation(gb_t[:, :, :].rearrange("p c t -> p (c t)"), ps[:, 0:2, :].rearrange("p b n -> p (b n)"),
                               ACT.Copy).then_inc(gb_ready, 1)
                if l == 0:
                    drain_ada(0, 4)
                ln_rows(2 * l)
                act.wait_ge(zc_mm, l + 1)
                act.activation(gc_t[:, :, :].rearrange("p c t -> p (c t)"), ps[:, 2:4, :].rearrange("p b n -> p (b n)"),
                               ACT.Copy).then_inc(gc_ready, 1)
                act.wait_ge(znt_mm, l + 1)
                for k in range(2):
                    act.activation(cq_t[:, k, :], ps[:, 4, k * T:(k + 1) * T], ACT.Copy, scale=prm_col(l, "q_norm_g", k))
                act.activation(ckv_t[:, :], ps[:, 5, 0:T], ACT.Copy, scale=prm_col(l, "kv_norm_g"))
                act.activation(kr_t[:, :, :].rearrange("p a t -> p (a t)"), ps[:, 6, :], ACT.Copy).then_inc(znt_ready, 1)
                for n in MIX_ADA[l][0] + MIX_ADA[l][1]:
                    drain_ada(l, n)
                act.wait_ge(qn_mm, l + 1)
                act.activation(qn_t[:, :, :].rearrange("p c t -> p (c t)"), ps[:, 2:4, :].rearrange("p b n -> p (b n)"),
                               ACT.Copy).then_inc(qn_ready, 1)
                act.wait_ge(v_mm, l + 1)
                act.activation(v_sb[:, :, :], ps[:, 0:2, :], ACT.Copy).then_inc(v_ready, 1)
                act.wait_ge(conv_ready, l + 1)
                act.activation(sq[:, :, :], cv[:, :, :], ACT.Square).then_inc(conv_sq, 1)
                act.wait_ge(bank7_full, bank7(("ssq_conv", l)) + 1)
                act.activation(gstd[:, 0, :], ps[:, 7, 0:TT], ACT.Sqrt, scale=1.0 / D_CONV,
                               bias=eps[:, 0:1]).then_inc(bank7_free, 1)
                for t in range(TT):
                    act.wait_ge(max_ready, TT * l + t + 1)
                    p = p0 if t == 0 else p1
                    for h in range(HEADS):
                        e = act.activation(p[:, h, :], p[:, h, :], ACT.Exp, scale=SCALE, bias=nmx[:, t, h:h + 1],
                                           accum_out=den[:, t, h:h + 1])
                    e.then_inc(exp_ready, 1)
                act.wait_ge(grr_ready, l + 1)
                if l >= 1:
                    act.wait_ge(x_ready, TT * 2 * l)
                for t in range(TT):
                    act.wait_ge(yc_mm, TT * l + t + 1)
                    for half, bank in enumerate(((0, 1), (3, 6))[t]):
                        e = act.activation(yv[:, t, half * 512:(half + 1) * 512], ps[:, bank, :], ACT.Copy,
                                           scale=grr[:, 0, t:t + 1])
                    e.then_inc(yc_ready, 1)
                for n in MIX_ADA[l][2]:
                    drain_ada(l, n)
                act.wait_ge(pt_mm, 3 * l + 1)
                act.activation(p_t0[:, :, 0:P], ps[:, 0, :].rearrange("p (h q) -> p h q", h=HEADS), ACT.Copy).then_inc(pt_ready, 1)
                act.wait_ge(pt_mm, 3 * l + 3)
                act.activation(p_t1[:, :, :], ps[:, 3, :].rearrange("p (h q) -> p h q", h=HEADS), ACT.Copy).then_inc(pt_ready, 1)
                act.wait_ge(attn_mm, l + 1)
                act.activation(sq[:, 0:2, :], ps[:, 2, :].rearrange("p (h q) -> p h q", h=2), ACT.Square)
                act.activation(sq[:, 2:4, :], ps[:, 4, :].rearrange("p (h q) -> p h q", h=2), ACT.Square).then_inc(attn_sq, 1)
                act.wait_ge(bank7_full, bank7(("ssq_attn", l)) + 1)
                act.activation(gstd[:, 1, :], ps[:, 7, 0:TT], ACT.Sqrt, scale=1.0 / 512,
                               bias=eps[:, 0:1]).then_inc(bank7_free, 1)
                layer_std(2 * l)

            mixer(0)

            def ff_silu(s):
                act.wait_ge(unit_used, ff_first_unit(s) + 4)
                if s >= 1:
                    act.wait_ge(hid_done, s)
                act.activation(sil[:, :], ps[:, 0, :], ACT.Silu).then_inc(silu_done, 1)

            def ff_hid(s):
                act.wait_ge(hid_done, s + 1)
                if s >= 1:
                    act.wait_ge(unit_used, ff_first_unit(s + 1))
                act.activation(hid_hi[:, :].rearrange("p (f n) -> p f n", f=4), hid, ACT.Copy).then_inc(hid_hi_ready, 1)

            def ff_unit(name, lo, u):
                if lo == 0:
                    wait_load(act, name)
                if u >= SRING:
                    act.wait_ge(unit_used, u - SRING + 1)
                act.activation(w_hi[:, u % SRING, :], slot_of(name)[:, lo:lo + UNIT], ACT.Copy).then_inc(unit_hi, 1)

            ff_unit(("gu", 0), 0, 0)
            modulate(1, 0, 2, ("ada", 0, 9))
            for s in range(FF_STEPS + 1):
                u = ff_first_unit(s)
                if s < FF_STEPS:
                    for k in range(1 if s == 0 else 0, 4):
                        ff_unit(("gu", s), k * UNIT, u + k)
                        if s >= 1 and k == 2:
                            ff_hid(s - 1)
                    if s >= 1:
                        drain_ada(*FF_ADA[s - 1][1:])
                    u += 4
                if s >= 1:
                    for k in range(2):
                        ff_unit(("dn", s - 1), k * UNIT, u + k)
                if s == FF_STEPS:
                    ff_hid(s - 1)
                    drain_ada(*FF_ADA[s - 1][1:])
                if s < FF_STEPS:
                    ff_silu(s)
                if s == 2:
                    ln_rows(1)
            layer_std(1)

            mixer(1)
            modulate(3, 1, 2, ("ada", 1, 9))

            def moe_hi(i, k):
                m = k // 4
                if k % 4 == 0:
                    act.wait_ge(slot_full[moe_slot(m)], moe_full(i, m))
                act.wait_ge(unit_used, i * E_UNITS + (FF_UNITS + k - SRING + 1))
                act.activation(w_hi[:, (FF_UNITS + k) % SRING, :],
                               raw[:, moe_slot(m), (k % 4) * UNIT:(k % 4 + 1) * UNIT], ACT.Copy).then_inc(unit_hi, 1)

            for k in range(HEAD):
                moe_hi(0, k)
            act.wait_ge(rel_ready, 1)
            act.activation(expo[:, :, :], expo[:, :, :], ACT.Exp).then_inc(expo_ready, 1)

            def gathered(i):
                act.wait_ge(xg_mm, i + 1)
                for c in range(KC // 2):
                    e = act.activation(xg[:, c, :], ps[:, 5, c * P:(c + 1) * P], ACT.Identity,
                                       scale=modc[:, 1, 3, c:c + 1], bias=modc[:, 1, 2, c:c + 1])
                e.then_inc(xg_ready, 1)
                act.wait_ge(xg_ready, i + 1)
                act.activation(xg_hi[:, 0:KC // 2, :], xg[:, 0:KC // 2, :], ACT.Copy).then_inc(xg_hi_ready, 1)

            gathered(0)
            ln_rows(3)

            def item(i, head, tail):
                after = {}
                for j in range(E_STEPS):
                    after.setdefault(moe_first_unit(j) + 6, []).insert(0, ("silu", j))
                    after.setdefault(moe_first_unit(j + 1) + 6 if j < E_STEPS - 1 else E_UNITS - 2, []).append(("hidt", j))
                for k in range(HEAD if head else 0, E_UNITS):
                    moe_hi(i, k)
                    for what, j in after.get(k, ()):
                        if what == "silu":
                            act.wait_ge(unit_used, i * E_UNITS + (FF_UNITS + moe_first_unit(j) + 4))
                            act.wait_ge(hid_done, i * E_STEPS + (FF_STEPS + j))
                            act.activation(sil[:, :], ps[:, GATE_BANKS[j % 2], :], ACT.Silu).then_inc(silu_done, 1)
                        else:
                            act.wait_ge(hidt_mm, i * E_STEPS + (j + 1))
                            act.activation(hid_hi[:, :], ps[:, 2, :], ACT.Copy).then_inc(hid_hi_ready, 1)
                gathered(i + 1)
                if tail:
                    moe_hi(i + 1, 0)
                    moe_hi(i + 1, 1)
                act.wait_ge(unit_used, i * E_UNITS + (FF_UNITS + E_UNITS))
                for half in range(2):
                    act.activation(y_hi[half], ps[:, 3 + half, :].rearrange("p (f n) -> p f n", f=4), ACT.Copy).then_inc(y_ready, 1)
                if tail:
                    moe_hi(i + 1, 2)
                    moe_hi(i + 1, 3)

            with act.Fori(0, E - 1) as i:
                item(i, True, True)
            item(E - 1, True, False)
            act.wait_ge(plan_ready, 1)
            n_items = act.value_load(plan_i[0:1, 0:1], min_val=E, max_val=ITEMS)
            for r in range(OVER):
                with act.If(n_items > E + r):
                    item(E + r, False, False)
            layer_std(3)

        @block.vector
        def _(dve):
            count = [0]

            def link(ins):
                count[0] += 1
                ins.then_inc(dve_order, 1)
                dve.wait_ge(dve_order, count[0])

            def ada_part(l, n, first, last):
                k, name = ADA_ORDER.index(("ada", l, n)), ("ada", l, n)
                w = slot_of(("ada", l, n)).rearrange("p (c n) -> p c n", c=KC)
                acc = ada_acc[:, k % 2, :]
                if first == 0:
                    if k < EARLY:
                        dve.wait_ge(half_full[k], 16)
                    else:
                        wait_load(dve, name)
                    if k >= 2:
                        dve.wait_ge(bank7_full, bank7(ADA_ORDER[k - 2]) + 1)
                for c in range(first, last):
                    if c == KC // 2 and k < EARLY:
                        wait_load(dve, name)
                    if c == 0:
                        ins = dve.tensor_scalar(acc, w[:, 0, :], c_act[:, 0:1], None, ALU.mult)
                    else:
                        ins = dve.scalar_tensor_tensor(acc, w[:, c, :], c_act[:, c:c + 1], acc, ALU.mult, ALU.add)
                    if c < KC - 1:
                        link(ins)
                    else:
                        ins.then_inc(ada_summed, 1)

            def ada(l, n):
                ada_part(l, n, 0, KC)

            def modulate(v, l, row, last):
                if v == 0:
                    dve.wait_ge(bank7_free, bank7(last) + 1)
                    shift, scale = modc[:, l, row, :], modc[:, l, row + 1, :]
                else:
                    shift, scale = modf[:, v, 0, :], modf[:, v, 1, :]
                for n, c0 in enumerate((2, 6)):
                    dve.wait_ge(xt_mm, KC * v + c0 + 2)
                    for c in (c0, c0 + 1):
                        dve.tensor_scalar(h_t[:, c, :], ps[:, c // 2, (c % 2) * T:(c % 2) * T + T],
                                          scale[:, c:c + 1], shift[:, c:c + 1], ALU.mult,
                                          ALU.add).then_inc(ht2_ready, 1)
                    if v == 1:
                        dve.wait_ge(ht2_ready, KC // 2 * v + 2 * n + 2)
                        link(dve.tensor_copy(h_hi[:, c0:c0 + 2, :], h_t[:, c0:c0 + 2, :]))
                        for c1 in (c0, c0 - 2):
                            if c1 == c0 - 2:
                                dve.wait_ge(h_hi_ready, n + 1)
                            dve.tensor_tensor(h_lo[:, c1:c1 + 2, :], h_t[:, c1:c1 + 2, :],
                                              h_hi[:, c1:c1 + 2, :].bitcast(F32), ALU.subtract).then_inc(h_lo_ready, 1)

            def fold(v):
                l, row, name = v // 2, 2 * (v % 2), ("ln1", "ln2")[(v - 1) % 2]
                dve.wait_ge(bank7_free, bank7(("ada", l, (3, 9)[v % 2])) + 1)
                scale = modc[:, l, row + 1, :]
                dve.tensor_tensor(modf[:, v, 1, :], prm_col((v - 1) // 2, name + "_g", 0, KC), scale, ALU.mult)
                link(dve.tensor_tensor(modf[:, v, 0, :], prm_col((v - 1) // 2, name + "_b", 0, KC), scale, ALU.mult))
                dve.tensor_tensor(modf[:, v, 0, :], modf[:, v, 0, :], modc[:, l, row, :], ALU.add).then_inc(fold_ready, 1)
                dve.wait_ge(fold_ready, v)

            def layer_norm(k, gated):
                for t in range(TT):
                    y = yv[:, t, :]
                    gated(t)
                    if k % 2:
                        link(dve.scalar_tensor_tensor(y, x_sb[:, t, :], ALPHA, y, ALU.mult, ALU.add))
                    for half in range(2):
                        ins = dve.bn_stats(stats[:, t, half, :], yv[:, t, half * 512:(half + 1) * 512])
                    link(ins)
                    dve.bn_aggr(meanvar[:, t, :], stats[:, t, :, :]).then_inc(var_ready, 1)
                for t in range(TT):
                    y = yv[:, t, :]
                    dve.wait_ge(var_ready, TT * k + t + 1)
                    dve.wait_ge(std_ready, TT * k + t + 1)
                    link(dve.reciprocal(rstd[:, t:t + 1], std[:, t:t + 1]))
                    ins = dve.tensor_scalar(y, y, meanvar[:, t, 0:1], rstd[:, t:t + 1], ALU.subtract, ALU.mult)
                    if k < 2 * L - 1:
                        ins.then_inc(xn_ready, 1)
                    else:
                        link(ins)
                        dve.wait_ge(ln_loaded, 32 * (k + 1))
                        link(dve.tensor_tensor(y, y, ln_g[:, :], ALU.mult))
                        dve.tensor_tensor(x_sb[:, t, :], y, ln_b[:, :], ALU.add).then_inc(x_ready, 1)

            dve.memset(cu[:, :, 0:2], 0.0)
            dve.wait_ge(consts, 1)
            dve.wait_ge(prm_loaded, 16 * PRM_LOADS)
            dve.tensor_copy(slot_no[:, :], slot_i[:, :])
            link(dve.tensor_copy(pos_f[:, :], pos_i[:, :]))
            for t in range(TT):
                for k in range(2):
                    ins = dve.tensor_scalar(ang[:, k, t, :], freq[:, :], pos_f[:, t:t + 1], None, ALU.mult)
            link(ins)
            link(dve.tensor_scalar(turns[:, 0], ang[:, 0], 1.0 / TWO_PI, 0.25, ALU.mult, ALU.add))
            link(dve.tensor_scalar(turns[:, 1], ang[:, 1], 1.0 / TWO_PI, None, ALU.mult))
            magic = 1.5 * 2.0 ** 23
            link(dve.tensor_scalar(turns[:], turns[:], magic, None, ALU.add))
            link(dve.tensor_scalar(turns[:], turns[:], -magic, None, ALU.add))
            for part in split2pi():
                link(dve.scalar_tensor_tensor(ang[:], turns[:], -part, ang[:], ALU.mult, ALU.add))
            link(dve.tensor_scalar(ang[:, 0], ang[:, 0], float(np.pi / 2), None, ALU.add))
            dve.tensor_scalar(ang[:], ang[:], 3.1415925, -3.1415925, ALU.min, ALU.max).then_inc(angles, 1)
            dve.wait_ge(bank7_free, 1)
            for n in range(4):
                ada(0, n)

            def rotate(dst1, dst2, x1, x2, cos, sin, tmp):
                dve.tensor_tensor(tmp[0], x1, cos, ALU.mult)
                dve.tensor_tensor(tmp[1], x2, sin, ALU.mult)
                dve.tensor_tensor(tmp[2], x2, cos, ALU.mult)
                link(dve.tensor_tensor(tmp[3], x1, sin, ALU.mult))
                dve.tensor_tensor(dst1, tmp[0], tmp[1], ALU.subtract)
                return dve.tensor_tensor(dst2, tmp[2], tmp[3], ALU.add)

            def mixer(l):
                modulate(2 * l, l, 0, ("ada", l, 3))
                dve.wait_ge(rms_ready, l + 1)
                link(dve.reciprocal(rrms[:, :, :], rms[:, :, :]))
                for t in range(TT):
                    dve.tensor_scalar(zn[:, t, 0:Q_LORA], ps[:, 4 + t, 0:Q_LORA], rrms[:, 0, t:t + 1], None, ALU.mult)
                    dve.tensor_scalar(zn[:, t, Q_LORA:], ps[:, 4 + t, Q_LORA:Q_LORA + KV_LORA],
                                      rrms[:, 1, t:t + 1], None, ALU.mult)
                if l == 0:
                    dve.wait_ge(trig_ready, 1)
                k0 = Q_LORA + KV_LORA
                link(dve.memset(kr[:, :, :, :, :], 0.0))
                link(rotate(kr[:, :, 0, 0, 0:HALF], kr[:, :, 0, 0, HALF:], ps[:, 4:6, k0:k0 + HALF],
                            ps[:, 4:6, k0 + HALF:k0 + ROPE], trig[:, 0], trig[:, 1], [rp_k[:, k] for k in range(4)]))
                dve.tensor_copy(kr[:, :, 1, 1, :], kr[:, :, 0, 0, :]).then_inc(zn_ready, 1)
                for n in ((4,) if l == 0 else ()) + MIX_ADA[l][0] + MIX_ADA[l][1]:
                    ada(l, n)
                dve.wait_ge(zu_mm, l + 1)
                dve.wait_ge(gc_ready, l + 1)
                dve.tensor_tensor(cu[:, :, 2:], ps[:, 0:2, :].rearrange("p b (c t) -> p (b c) t", c=2), gc_t[:, :, :],
                                  ALU.mult).then_inc(cu_ready, 1)
                dve.wait_ge(qr_mm, l + 1)
                q = ps[:, 6, :].rearrange("p (t h r) -> p t h r", t=TT, h=HEADS)
                for t in range(TT):
                    cos = trig[:, 0, t:t + 1, :].to_broadcast([P, HEADS, HALF])
                    sin = trig[:, 1, t:t + 1, :].to_broadcast([P, HEADS, HALF])
                    ins = rotate(qr[:, t, :, 0:HALF], qr[:, t, :, HALF:], q[:, t, :, 0:HALF], q[:, t, :, HALF:],
                                 cos, sin, [rp_q[:, k, t] for k in range(4)])
                ins.then_inc(qr_ready, 1)
                dve.wait_ge(kn_mm, l + 1)
                dve.tensor_copy(kn_t[:, :, :].rearrange("p c t -> p (c t)"),
                                ps[:, 4:6, :].rearrange("p b n -> p (b n)")).then_inc(kn_ready, 1)
                dve.wait_ge(qrt_mm, l + 1)
                dve.tensor_copy(qr_t[:, :, :].rearrange("p c t -> p (c t)"), ps[:, 6, :]).then_inc(qrt_ready, 1)
                dve.wait_ge(cu_ready, l + 1)
                dve.wait_ge(qr_ready, l + 1)
                for c in range(CC):
                    dve.tensor_scalar(cv[:, c, :], cu[:, c, 2:], prm_col(l, "conv_w", 2 * CC + c), None, ALU.mult).then_inc(dve_order, 1)
                count[0] += CC
                for j in (1, 0):
                    dve.wait_ge(dve_order, count[0])
                    for c in range(CC):
                        dve.scalar_tensor_tensor(cv[:, c, :], cu[:, c, j:j + T], prm_col(l, "conv_w", j * CC + c),
                                                 cv[:, c, :], ALU.mult, ALU.add).then_inc(dve_order, 1)
                    count[0] += CC
                dve.wait_ge(dve_order, count[0])
                dve.wait_ge(gb_ready, l + 1)
                dve.tensor_tensor(cv[:, :, :], cv[:, :, :], gb_t[:, :, :], ALU.mult).then_inc(conv_ready, 1)
                dve.wait_ge(conv_ready, l + 1)
                for c in range(CC):
                    ins = dve.tensor_scalar(cv_t[:, c, :], cv[:, c, :], prm_col(l, "mix_norm_g", 4 + c), None, ALU.mult)
                ins.then_inc(conv_scaled, 1)
                for n in MIX_ADA[l][2]:
                    ada(l, n)
                dve.wait_ge(score_mm, TT * l + 1)
                mask = causal[:, :].rearrange("p (a s) -> p a s", a=1).to_broadcast([P, HEADS, P])
                link(dve.tensor_tensor(p0[:, :, :], ps[:, 2, :].rearrange("p (h s) -> p h s", h=HEADS), mask, ALU.add))
                link(dve.tensor_reduce(mx[:, 0, :], p0[:, :, :], AX_X, ALU.max))
                dve.tensor_scalar(nmx[:, 0, :], mx[:, 0, :], -SCALE, None, ALU.mult).then_inc(max_ready, 1)
                dve.wait_ge(score_mm, TT * l + 2)
                s1 = ps[:, 4:6, :].rearrange("p b (h s) -> p (b h) s", h=2)
                dve.tensor_copy(p1[:, :, 0:P], s1[:, :, 0:P])
                link(dve.tensor_tensor(p1[:, :, P:T], s1[:, :, P:T], mask, ALU.add))
                link(dve.tensor_reduce(mx[:, 1, :], p1[:, :, :], AX_X, ALU.max))
                dve.tensor_scalar(nmx[:, 1, :], mx[:, 1, :], -SCALE, None, ALU.mult).then_inc(max_ready, 1)
                dve.wait_ge(bank7_free, bank7(("ssq_conv", l)) + 1)
                dve.reciprocal(grr[:, 0, :], gstd[:, 0, :]).then_inc(grr_ready, 1)
                for t in range(TT):
                    dve.wait_ge(exp_ready, TT * l + t + 1)
                    link(dve.reciprocal(rden[:, t, :], den[:, t, :]))
                    p = p0 if t == 0 else p1
                    for h in range(HEADS):
                        ins = dve.tensor_scalar(p[:, h, :], p[:, h, :], rden[:, t, h:h + 1], None, ALU.mult)
                    ins.then_inc(prob_ready, 1)
                dve.wait_ge(pt_mm, 3 * l + 2)
                dve.tensor_copy(p_t0[:, :, P:T], ps[:, 1, :].rearrange("p (h q) -> p h q", h=HEADS)).then_inc(pt_ready, 1)
                dve.wait_ge(attn_mm, l + 1)
                dve.wait_ge(attn_sq, l + 1)
                for h in range(HEADS):
                    ins = dve.tensor_scalar(a_t[:, h, :], ps[:, 2 + 2 * (h // 2), (h % 2) * T:(h % 2 + 1) * T],
                                            prm_col(l, "mix_norm_g", h), None, ALU.mult)
                ins.then_inc(attn_scaled, 1)
                dve.wait_ge(yc_ready, TT * (l + 1))
                if l >= 1:
                    dve.wait_ge(x_ready, TT * 2 * l)
                dve.wait_ge(bank7_free, bank7(("ada", l, 5)) + 1)
                for t in range(TT):
                    link(dve.tensor_tensor(yv[:, t, :], yv[:, t, :], gate1[:, :], ALU.mult))
                    link(dve.scalar_tensor_tensor(yv[:, t, :], x_sb[:, t, :], ALPHA, yv[:, t, :], ALU.mult, ALU.add))
                dve.wait_ge(bank7_free, bank7(("ssq_attn", l)) + 1)
                link(dve.reciprocal(grr[:, 1, :], gstd[:, 1, :]))
                def gated(t):
                    dve.wait_ge(ya_mm, TT * l + t + 1)
                    b = (0, 5)[t]
                    tmp = att_tmp[t]
                    link(dve.scalar_tensor_tensor(tmp, ps[:, b:b + 2, :].rearrange("p b n -> p (b n)"),
                                                  grr[:, 1, t:t + 1], gate1[:, :], ALU.mult, ALU.mult))
                    link(dve.tensor_tensor(yv[:, t, :], yv[:, t, :], tmp, ALU.add))

                fold(2 * l + 1)
                layer_norm(2 * l, gated)

            dve.wait_ge(x_loaded, 16 * TT)
            mixer(0)

            def ff_unit(name, lo, u):
                dve.wait_ge(unit_hi, u + 1)
                dve.tensor_tensor(w_lo[:, u % SRING, :], slot_of(name)[:, lo:lo + UNIT],
                                  w_hi[:, u % SRING, :].bitcast(F32), ALU.subtract).then_inc(unit_lo, 1)

            def hidden(n):
                dve.wait_ge(silu_done, n + 1)
                dve.tensor_tensor(hid, ps[:, 1, :].rearrange("p (f n) -> p f n", f=4),
                                  sil[:, :].rearrange("p (f n) -> p f n", f=4), ALU.mult).then_inc(hid_done, 1)

            def hidden_lo(n, value):
                dve.wait_ge(hid_hi_ready, n + 1)
                dve.tensor_tensor(hid_lo[:, :].rearrange("p (f n) -> p f n", f=4), value,
                                  hid_hi[:, :].bitcast(F32).rearrange("p (f n) -> p f n", f=4),
                                  ALU.subtract).then_inc(hid_lo_ready, 1)

            ff_unit(("gu", 0), 0, 0)
            modulate(1, 0, 2, ("ada", 0, 9))
            for s in range(FF_STEPS + 1):
                u = ff_first_unit(s)
                if s < FF_STEPS:
                    for k in range(4):
                        if u + k > 0:
                            ff_unit(("gu", s), k * UNIT, u + k)
                        if s >= 1 and k == 2:
                            hidden_lo(s - 1, hid)
                        ada_part(*FF_ADA[s][1:], 2 * k, 2 * k + 2)
                    u += 4
                if s >= 1:
                    for k in range(2):
                        ff_unit(("dn", s - 1), k * UNIT, u + k)
                if s < FF_STEPS:
                    if s >= 1:
                        dve.wait_ge(hid_lo_ready, s)
                    hidden(s)
                else:
                    hidden_lo(s - 1, hid)

            dve.wait_ge(unit_used, FF_UNITS)
            dve.wait_ge(bank7_free, bank7(("ada", 0, 11)) + 1)

            def gated_ff(t):
                link(dve.tensor_tensor(yv[:, t, :], ps[:, 3 + 2 * t:5 + 2 * t, :].rearrange("p b n -> p (b n)"),
                                       gate2[:, :], ALU.mult))

            fold(2)
            dve.wait_ge(x_ready, TT)
            layer_norm(1, gated_ff)

            dve.memset(cu[:, :, 0:2], 0.0)
            mixer(1)
            modulate(3, 1, 2, ("ada", 1, 9))

            def moe_lo(i, k):
                m = k // 4
                q = (FF_UNITS + k) % SRING
                dve.wait_ge(unit_hi, i * E_UNITS + (FF_UNITS + k + 1))
                dve.tensor_tensor(w_lo[:, q, :], raw[:, moe_slot(m), (k % 4) * UNIT:(k % 4 + 1) * UNIT],
                                  w_hi[:, q, :].bitcast(F32), ALU.subtract).then_inc(unit_lo, 1)

            for ap in (pads[:], cnt[:]):
                dve.memset(ap, 0.0)
            dve.memset(place[:, :, ITEMS:], -1.0)
            dve.memset(share[:, :, ITEMS:], 0.0)
            dve.tensor_copy(e_no[:, :], slot_no[:, 0:E])
            for k in range(HEAD):
                moe_lo(0, k)
            dve.wait_ge(logit_mm, 1)
            link(dve.tensor_copy(logit[:, :, :], ps[:, 4, 0:TT * E].rearrange("p (t e) -> p t e", t=TT)))
            for t in range(TT):
                ins = dve.max(top[:, t, :], logit[:, t, :])
            link(ins)
            for t in range(TT):
                dve.tensor_scalar(expo[:, t, :], logit[:, t, :], top[:, t, 0:1], None, ALU.subtract).then_inc(rel_ready, 1) \
                    if t == TT - 1 else dve.tensor_scalar(expo[:, t, :], logit[:, t, :], top[:, t, 0:1], None, ALU.subtract)
                dve.tensor_scalar(above[:, t, :], logit[:, t, :], top[:, t, 1:2], None, ALU.is_gt)
                ins = dve.tensor_scalar(pads[:, 0, t, E:], logit[:, t, :], top[:, t, 1:2], None, ALU.is_equal)
            link(ins)

            def prefix(p, q, r, shape_of):
                link(dve.tensor_tensor(shape_of(q, 0), shape_of(p, 0), shape_of(p, 1), ALU.add))
                link(dve.tensor_tensor(shape_of(r, 0), shape_of(q, 0), shape_of(q, 2), ALU.add))
                link(dve.tensor_tensor(shape_of(q, 0), shape_of(r, 0), shape_of(r, 4), ALU.add))

            prefix(0, 1, 2, lambda k, back: pads[:, k, :, E - back:2 * E - back])
            link(dve.tensor_reduce(n_above[:, :], above[:, :, :], AX_X, ALU.add))
            link(dve.tensor_scalar(n_above[:, :], n_above[:, :], -1.0, 2.0, ALU.mult, ALU.add))
            for t in range(TT):
                ins = dve.scalar_tensor_tensor(chosen[:, t, :], pads[:, 1, t, E:], n_above[:, t:t + 1],
                                               pads[:, 0, t, E:], ALU.is_le, ALU.mult)
            link(ins)
            dve.tensor_tensor(chosen[:, :, :], chosen[:, :, :], above[:, :, :], ALU.add).then_inc(chosen_ready, 1)
            dve.wait_ge(chosen_ready, 1)
            dve.wait_ge(expo_ready, 1)
            link(dve.tensor_tensor(expo[:, :, :], expo[:, :, :], chosen[:, :, :], ALU.mult))
            link(dve.tensor_reduce(exsum[:, :], expo[:, :, :], AX_X, ALU.add))
            link(dve.reciprocal(exinv[:, :], exsum[:, :]))
            for t in range(TT):
                ins = dve.tensor_scalar(share[:, t, 0:E], expo[:, t, :], exinv[:, t:t + 1], None, ALU.mult)
            link(ins)
            dve.wait_ge(place_mm, 1)
            pos = ps[:, 4, 64:64 + TT * E].rearrange("p (t e) -> p t e", t=TT)
            link(dve.scalar_tensor_tensor(place[:, :, 0:E], pos, 1.0, chosen[:, :, :], ALU.add, ALU.mult))
            link(dve.tensor_scalar(place[:, :, 0:E], place[:, :, 0:E], -1.0, None, ALU.add))

            def build_sel(i):
                for t in range(TT):
                    ins = dve.tensor_scalar(sel[:, t, :], slot_no[:, :], place[:, t, bass.ds(i, 1)], None, ALU.is_equal)
                ins.then_inc(sel_ready, 1)

            link(dve.tensor_scalar(cnt[:, 0, E:], ps[:, 4, 64 + TT * E:64 + TT * E + E], float(P), None, ALU.is_gt))
            build_sel(0)
            prefix(0, 1, 2, lambda k, back: cnt[:, k, E - back:2 * E - back])
            link(dve.tensor_tensor(rank[:, :], cnt[:, 1, E:], cnt[:, 0, E:], ALU.subtract))
            for r in range(OVER):
                ins = dve.scalar_tensor_tensor(pick[:, r, :], rank[:, :], float(r), cnt[:, 0, E:], ALU.is_equal, ALU.mult)
            link(ins)
            for r in range(OVER):
                for t in range(TT):
                    dve.scalar_tensor_tensor(picked[:, r, t, :], place[:, t, 0:E], float(1 - P), pick[:, r, :],
                                             ALU.add, ALU.mult)
                    dve.tensor_tensor(picked[:, r, TT + t, :], share[:, t, 0:E], pick[:, r, :], ALU.mult)
                ins = dve.tensor_tensor(picked[:, r, 4, :], e_no[:, :], pick[:, r, :], ALU.mult)
            link(ins)
            for r in range(OVER):
                for t in range(TT):
                    dve.tensor_reduce(place[:, t, E + r:E + r + 1], picked[:, r, t, :], AX_X, ALU.add)
                    dve.tensor_reduce(share[:, t, E + r:E + r + 1], picked[:, r, TT + t, :], AX_X, ALU.add)
                dve.tensor_reduce(plan_f[:, 1 + r:2 + r], picked[:, r, 4, :], AX_X, ALU.add)
            link(dve.tensor_reduce(plan_f[:, 0:1], cnt[:, 0, E:], AX_X, ALU.add))
            link(dve.tensor_scalar(place[:, :, E:ITEMS], place[:, :, E:ITEMS], -1.0, None, ALU.add))
            link(dve.tensor_scalar(plan_f[:, 0:1], plan_f[:, 0:1], float(E), None, ALU.add))
            dve.tensor_copy(plan_i[:, :], plan_f[:, :]).then_inc(plan_ready, 1)

            def gathered(i):
                half = slice(KC // 2, KC)
                dve.wait_ge(xg_mm, i + 1)
                for c in range(KC // 2, KC):
                    ins = dve.tensor_scalar(xg[:, c, :], ps[:, 6, (c - 4) * P:(c - 3) * P], modc[:, 1, 3, c:c + 1],
                                            modc[:, 1, 2, c:c + 1], ALU.mult, ALU.add)
                ins.then_inc(xg2_ready, 1)
                dve.wait_ge(xg2_ready, i + 1)
                dve.tensor_copy(xg_hi[:, half, :], xg[:, half, :]).then_inc(xg2_hi, 1)
                dve.wait_ge(xg2_hi, i + 1)
                dve.tensor_tensor(xg_lo[:, half, :], xg[:, half, :], xg_hi[:, half, :].bitcast(F32), ALU.subtract)
                dve.wait_ge(xg_hi_ready, i + 1)
                half = slice(0, KC // 2)
                dve.tensor_tensor(xg_lo[:, half, :], xg[:, half, :], xg_hi[:, half, :].bitcast(F32),
                                  ALU.subtract).then_inc(xg_lo_ready, 1)

            gathered(0)
            dve.wait_ge(plan_ready, 1)

            def item(i, head, tail):
                after = {}
                for j in range(E_STEPS):
                    after.setdefault(moe_first_unit(j) + 9, []).append(("hid", j))
                    after.setdefault(moe_first_unit(j + 1) + 6 if j < E_STEPS - 1 else E_UNITS - 2, []).append(("hidt", j))
                for k in range(HEAD if head else 0, E_UNITS):
                    moe_lo(i, k)
                    for what, j in after.get(k, ()):
                        if what == "hid":
                            dve.wait_ge(unit_used, i * E_UNITS + (FF_UNITS + moe_first_unit(j) + 8))
                            hidden(i * E_STEPS + (FF_STEPS + j))
                        else:
                            hidden_lo(i * E_STEPS + (FF_STEPS + j), ps[:, 2, :].rearrange("p (f n) -> p f n", f=4))
                    if k == 16:
                        dve.wait_ge(selt_mm, i + 1)
                        dve.tensor_copy(sel_t, ps[:, 5, 0:T].rearrange("p (t n) -> p t n", t=TT)).then_inc(selt_ready, 1)
                        build_sel(i + 1)
                gathered(i + 1)
                if tail:
                    moe_lo(i + 1, 0)
                    moe_lo(i + 1, 1)
                for half in range(2):
                    dve.wait_ge(y_ready, i * 2 + (half + 1))
                    dve.tensor_tensor(y_lo[half][:, :].rearrange("p (f n) -> p f n", f=4),
                                      ps[:, 3 + half, :].rearrange("p (f n) -> p f n", f=4), y_hi[half].bitcast(F32),
                                      ALU.subtract).then_inc(y_lo_ready, 1)
                if tail:
                    moe_lo(i + 1, 2)
                for half in range(2):
                    for t in range(TT):
                        dve.wait_ge(scatter_mm, i * 4 + (2 * half + t + 1))
                        dve.wait_ge(acc_ready, i * 4 + 1)
                        acc = moe_acc[:, t, half * 512:(half + 1) * 512]
                        dve.scalar_tensor_tensor(acc, ps[:, SCATTER_BANKS[t][half], :], share[:, t, bass.ds(i, 1)], acc,
                                                 ALU.mult, ALU.add).then_inc(acc_ready, 1)
                    if tail and half == 0:
                        moe_lo(i + 1, 3)

            dve.wait_ge(x_ready, TT * (2 * L - 1))
            dve.memset(moe_acc[:, :, :], 0.0).then_inc(acc_ready, 1)
            with dve.Fori(0, E - 1) as i:
                item(i, True, True)
            item(E - 1, True, False)
            n_items = dve.value_load(plan_i[0:1, 0:1], min_val=E, max_val=ITEMS)
            for r in range(OVER):
                with dve.If(n_items > E + r):
                    item(E + r, False, False)
            link(dve.memset(n_above[:, :], 0.0))
            dve.wait_ge(bank7_free, bank7(("ada", 1, 11)) + 1)

            def gated_moe(t):
                link(dve.tensor_tensor(yv[:, t, :], moe_acc[:, t, :], gate2[:, :], ALU.mult))

            layer_norm(3, gated_moe)

        @block.tensor
        def _(pe):
            def use_bank7(use):
                k = bank7(use)
                if k >= 1:
                    pe.wait_ge(bank7_free, k)

            def ada(l, n):
                k = ADA_ORDER.index(("ada", l, n))
                pe.wait_ge(ada_summed, k + 1)
                use_bank7(("ada", l, n))
                acc = ada_acc[:, k % 2, :]
                if n // 2 in (2, 5):
                    pe.matmul(ps[:, 7, :], ones[:, :], acc, start=True, stop=False)
                    m = pe.matmul(ps[:, 7, :], ident[0:STRIPS, n:n + 1].to_broadcast([STRIPS, P]),
                                  ada_bias[:, l, :], start=False, stop=True)
                else:
                    for c in range(4):
                        cols = slice(c * P, (c + 1) * P)
                        pe.matmul(ps[:, 7, c:c + 1], acc[:, cols], ones[:, 0:1], start=True, stop=False)
                        m = pe.matmul(ps[:, 7, c:c + 1], ada_bias[:, l, cols], ident[0:STRIPS, n:n + 1],
                                      start=False, stop=True)
                m.then_inc(bank7_full, 1)

            def turn_input(v):
                x = yv if v >= 1 else x_sb
                if v >= 1:
                    pe.wait_ge(xn_ready, TT * v)
                else:
                    pe.wait_ge(x_loaded, 16 * TT)
                for c in range(KC):
                    for t in range(TT):
                        o = (c % 2) * T + t * P
                        m = pe.transpose(ps[:, c // 2, o:o + P], x[:, t, c * P:(c + 1) * P], ident[:, :])
                    m.then_inc(xt_mm, 1)

            pe.wait_ge(consts, 1)
            pe.wait_ge(prm_loaded, 16 * PRM_LOADS)
            pe.transpose(ps[:, 7, 0:PRM], prm_rows[:, :], ident[0:PRM, 0:PRM]).then_inc(bank7_full, 1)
            for n in range(4):
                ada(0, n)

            def mixer(l):
                turn_input(2 * l)
                wait_load(pe, ("wa", l))
                pe.wait_ge(ht_ready, KC // 2 * (2 * l + 1))
                pe.wait_ge(ht2_ready, KC // 2 * (2 * l + 1))
                wa = slot_of(("wa", l))[:, 0:KC * ZA].rearrange("p (c n) -> p c n", c=KC)
                for t in range(TT):
                    for c in range(KC):
                        m = pe.matmul(ps[:, 4 + t, 0:ZA], h_t[:, c, t * P:(t + 1) * P], wa[:, c, :],
                                      start=(c == 0), stop=(c == KC - 1))
                    m.then_inc(za_mm, 1)

                def channels(name, bank):
                    wait_load(pe, name)
                    w = slot_of(name).rearrange("p (c n) -> p c n", c=KC)
                    for n in range(CC):
                        for c in range(KC):
                            m = pe.matmul(ps[:, bank + n // 2, (n % 2) * T:(n % 2 + 1) * T],
                                          w[:, c, n * P:(n + 1) * P], h_t[:, c, :], start=(c == 0), stop=(c == KC - 1))
                    return m

                channels(("wb", l), 0).then_inc(zb_mm, 1)
                if l == 0:
                    ada(0, 4)
                channels(("wc", l), 2).then_inc(zc_mm, 1)
                pe.wait_ge(zn_ready, l + 1)
                for k in range(2):
                    for t in range(TT):
                        pe.transpose(ps[:, 4, k * T + t * P:k * T + (t + 1) * P], zn[:, t, k * P:(k + 1) * P], ident[:, :])
                for t in range(TT):
                    pe.transpose(ps[:, 5, t * P:(t + 1) * P], zn[:, t, Q_LORA:], ident[:, :])
                    for k in range(2):
                        m = pe.transpose(ps[:, 6, k * T + t * P:k * T + (t + 1) * P],
                                         kr[:, t, k, :, :].rearrange("p a r -> p (a r)"), ident[:, :])
                m.then_inc(znt_mm, 1)
                for n in MIX_ADA[l][0]:
                    ada(l, n)
                pe.wait_ge(gb_ready, l + 1)
                channels(("wu", l), 0).then_inc(zu_mm, 1)
                for n in MIX_ADA[l][1]:
                    ada(l, n)
                wait_load(pe, ("qkv", l))
                uq = slot_of(("qkv", l))[:, 0:2 * 768].rearrange("p (c h n) -> p c h n", c=2, h=HEADS)
                ukv = slot_of(("qkv", l))[:, 2 * 768:2 * 768 + 1024].rearrange("p (h n) -> p h n", h=HEADS)
                pe.wait_ge(znt_ready, l + 1)
                for t in range(TT):
                    for c in range(2):
                        m = pe.matmul(ps[:, 6, t * T:(t + 1) * T], cq_t[:, c, t * P:(t + 1) * P], uq[:, c, :, NOPE:],
                                      start=(c == 0), stop=(c == 1))
                m.then_inc(qr_mm, 1)
                pe.wait_ge(gc_ready, l + 1)
                for h in range(HEADS):
                    for c in range(2):
                        m = pe.matmul(ps[:, 2 + h // 2, (h % 2) * T:(h % 2 + 1) * T], uq[:, c, h, 0:NOPE], cq_t[:, c, :],
                                      start=(c == 0), stop=(c == 1))
                m.then_inc(qn_mm, 1)
                for h in range(HEADS):
                    m = pe.matmul(ps[:, 4 + h // 2, (h % 2) * T:(h % 2 + 1) * T], ukv[:, h, 0:NOPE], ckv_t[:, :],
                                  start=True, stop=True)
                m.then_inc(kn_mm, 1)
                pe.wait_ge(cu_ready, l + 1)
                for t in range(TT):
                    m = pe.matmul(ps[:, t, :], ckv_t[:, t * P:(t + 1) * P], ukv[:, :, NOPE:], start=True, stop=True)
                m.then_inc(v_mm, 1)
                pe.wait_ge(qr_ready, l + 1)
                for k in range(2):
                    for t in range(TT):
                        m = pe.transpose(ps[:, 6, k * T + t * P:k * T + (t + 1) * P],
                                         qr[:, t, 2 * k:2 * k + 2, :].rearrange("p h r -> p (h r)"), ident[:, :])
                m.then_inc(qrt_mm, 1)
                pe.wait_ge(qn_ready, l + 1)
                pe.wait_ge(kn_ready, l + 1)
                pe.wait_ge(qrt_ready, l + 1)
                for t in range(TT):
                    keys = P * (t + 1)
                    for h in range(HEADS):
                        o = ps[:, 2, h * P:(h + 1) * P] if t == 0 else ps[:, 4 + h // 2, (h % 2) * T:(h % 2 + 1) * T]
                        pe.matmul(o, qn_t[:, h, t * P:(t + 1) * P], kn_t[:, h, 0:keys], start=True, stop=False)
                        m = pe.matmul(o, qr_t[:, h // 2, t * P:(t + 1) * P], kr_t[:, h % 2, 0:keys],
                                      start=False, stop=True)
                    m.then_inc(score_mm, 1)
                pe.wait_ge(conv_sq, l + 1)
                use_bank7(("ssq_conv", l))
                for t in range(TT):
                    for c in range(CC):
                        m = pe.matmul(ps[:, 7, t:t + 1], sq[:, c, t * P:(t + 1) * P], ones[:, 0:1],
                                      start=(c == 0), stop=(c == CC - 1))
                m.then_inc(bank7_full, 1)
                pe.wait_ge(conv_scaled, l + 1)
                pe.wait_ge(v_ready, l + 1)
                wait_load(pe, ("oc", l))
                oc = slot_of(("oc", l)).rearrange("p (c n) -> p c n", c=4)
                for t in range(TT):
                    for half, bank in enumerate(((0, 1), (3, 6))[t]):
                        for c in range(CC):
                            m = pe.matmul(ps[:, bank, :], cv_t[:, c, t * P:(t + 1) * P], oc[:, c, half * 512:(half + 1) * 512],
                                          start=(c == 0), stop=(c == CC - 1))
                    m.then_inc(yc_mm, 1)
                for n in MIX_ADA[l][2]:
                    ada(l, n)
                pe.wait_ge(prob_ready, TT * l + 1)
                pe.wait_ge(yc_ready, TT * l + 1)
                for h in range(HEADS):
                    m = pe.transpose(ps[:, 0, h * P:(h + 1) * P], p0[:, h, :], ident[:, :])
                m.then_inc(pt_mm, 1)
                pe.wait_ge(prob_ready, TT * l + 2)
                pe.wait_ge(yc_ready, TT * l + 2)
                for bank, s in ((1, 0), (3, 1)):
                    for h in range(HEADS):
                        m = pe.transpose(ps[:, bank, h * P:(h + 1) * P], p1[:, h, s * P:(s + 1) * P], ident[:, :])
                    m.then_inc(pt_mm, 1)
                pe.wait_ge(pt_ready, 3 * (l + 1))
                for h in range(HEADS):
                    bank, o = 2 + 2 * (h // 2), (h % 2) * T
                    pe.matmul(ps[:, bank, o:o + T], v_sb[:, 0, h * VH:(h + 1) * VH], p_t0[:, h, :], start=True, stop=False)
                    m = pe.matmul(ps[:, bank, o + P:o + T], v_sb[:, 1, h * VH:(h + 1) * VH], p_t1[:, h, :], start=False, stop=True)
                m.then_inc(attn_mm, 1)
                pe.wait_ge(attn_sq, l + 1)
                use_bank7(("ssq_attn", l))
                for t in range(TT):
                    for c in range(HEADS):
                        m = pe.matmul(ps[:, 7, t:t + 1], sq[:, c, t * P:(t + 1) * P], ones[:, 0:1],
                                      start=(c == 0), stop=(c == HEADS - 1))
                m.then_inc(bank7_full, 1)
                pe.wait_ge(attn_scaled, l + 1)
                wait_load(pe, ("oa", l))
                oa = slot_of(("oa", l)).rearrange("p (c n) -> p c n", c=4)
                for t in range(TT):
                    for half in range(2):
                        for c in range(4):
                            m = pe.matmul(ps[:, (0, 5)[t] + half, :], a_t[:, c, t * P:(t + 1) * P],
                                          oa[:, c, half * 512:(half + 1) * 512], start=(c == 0), stop=(c == 3))
                    m.then_inc(ya_mm, 1)

            def three(o, x_hi, x_lo, hi, lo, first, last):
                pe.matmul(o, x_lo, hi, start=first, stop=False, skip_group_check=True)
                pe.matmul(o, x_hi, lo, start=False, stop=False, skip_group_check=True)
                return pe.matmul(o, x_hi, hi, start=False, stop=last, skip_group_check=True)

            mixer(0)
            turn_input(1)

            def ff_rows(s, what, bank):
                for k in range(2):
                    if s == 0 and what == 0:
                        pe.wait_ge(h_lo_ready, 2 * k + 2)
                    u = ff_first_unit(s) + 2 * what + k
                    pe.wait_ge(unit_lo, u + 1)
                    hi = w_hi[:, u % SRING, :].rearrange("p (c n) -> p c n", c=4)
                    lo = w_lo[:, u % SRING, :].rearrange("p (c n) -> p c n", c=4)
                    for f in range(2):
                        for c in range(4):
                            cc, cols = 4 * k + c, slice(f * P, (f + 1) * P)
                            m = three(ps[:, bank, f * T:(f + 1) * T], hi[:, c, cols], lo[:, c, cols],
                                      h_hi[:, cc, :], h_lo[:, cc, :], k == 0 and f == 0 and c == 0,
                                      k == 1 and f == 1 and c == 3)
                    m.then_inc(unit_used, 1)

            def ff_down(s):
                pe.wait_ge(hid_lo_ready, s + 1)
                for f in range(2):
                    u = (ff_first_unit(s + 1) + 4 if s < FF_STEPS - 1 else FF_UNITS - 2) + f
                    pe.wait_ge(unit_lo, u + 1)
                    for t in range(TT):
                        x = slice(f * T + t * P, f * T + (t + 1) * P)
                        for half in range(2):
                            cols = slice(half * 512, (half + 1) * 512)
                            m = three(ps[:, 3 + 2 * t + half, :], hid_hi[:, x], hid_lo[:, x], w_hi[:, u % SRING, cols],
                                      w_lo[:, u % SRING, cols], s == 0 and f == 0, s == FF_STEPS - 1 and f == 1)
                    m.then_inc(unit_used, 1)

            for s in range(FF_STEPS + 1):
                if s < FF_STEPS:
                    if s >= 1:
                        ada(*FF_ADA[s - 1][1:])
                        pe.wait_ge(silu_done, s)
                    ff_rows(s, 0, 0)
                    if s >= 1:
                        pe.wait_ge(hid_done, s)
                    ff_rows(s, 1, 1)
                else:
                    ada(*FF_ADA[s - 1][1:])
                if s >= 1:
                    ff_down(s - 1)

            mixer(1)
            turn_input(3)
            pe.wait_ge(ht_ready, 2 * KC)
            pe.wait_ge(ht2_ready, 2 * KC)
            pe.wait_ge(rt_loaded, 32)
            for t in range(TT):
                o = ps[:, 4, t * E:(t + 1) * E]
                for c in range(KC):
                    pe.matmul(o, h_t[:, c, t * P:(t + 1) * P], router_w[:, c, :], start=(c == 0), stop=False)
                m = pe.matmul(o, ones[0:1, :], router_b[:, :], start=False, stop=True)
            m.then_inc(logit_mm, 1)
            pe.wait_ge(chosen_ready, 1)
            pe.matmul(ps[:, 4, 64:64 + E], before[:, :], chosen[:, 0, :], start=True, stop=True)
            pe.matmul(ps[:, 4, 64 + E:64 + 2 * E], before[:, :], chosen[:, 1, :], start=True, stop=False)
            pe.matmul(ps[:, 4, 64 + E:64 + 2 * E], ones[:, :], chosen[:, 0, :], start=False, stop=True)
            pe.matmul(ps[:, 4, 64 + 2 * E:64 + 3 * E], ones[:, :], chosen[:, 0, :], start=True, stop=False)
            pe.matmul(ps[:, 4, 64 + 2 * E:64 + 3 * E], ones[:, :], chosen[:, 1, :], start=False, stop=True).then_inc(place_mm, 1)

            def gather(i):
                pe.wait_ge(sel_ready, i + 1)
                for c in range(KC):
                    for t in range(TT):
                        m = pe.matmul(ps[:, 5 + c // 4, (c % 4) * P:(c % 4 + 1) * P], x_sb[:, t, c * P:(c + 1) * P],
                                      sel[:, t, :], start=(t == 0), stop=(t == TT - 1))
                m.then_inc(xg_mm, 1)

            pe.wait_ge(bank7_free, len(BANK7))
            pe.wait_ge(x_ready, TT * (2 * L - 1))
            gather(0)

            def item(i):
                units, steps = i * E_UNITS, i * E_STEPS

                def unit(k):
                    pe.wait_ge(unit_lo, units + (FF_UNITS + k + 1))
                    return (FF_UNITS + k) % SRING

                def rows(j, what, bank):
                    for k in range(4):
                        q = unit(moe_first_unit(j) + 4 * what + k)
                        for c in range(2):
                            cols = slice(c * 512, (c + 1) * 512)
                            cc = 2 * k + c
                            m = three(ps[:, bank, :], xg_hi[:, cc, :], xg_lo[:, cc, :], w_hi[:, q, cols], w_lo[:, q, cols],
                                      cc == 0, cc == KC - 1)
                        m.then_inc(unit_used, 1)

                def turn(j):
                    pe.wait_ge(hid_done, steps + (FF_STEPS + j + 1))
                    pe.wait_ge(hid_lo_ready, steps + (FF_STEPS + j))
                    for f in range(4):
                        m = pe.transpose(ps[:, 2, f * P:(f + 1) * P], hid[:, f, :], ident[:, :])
                    m.then_inc(hidt_mm, 1)

                def down(j):
                    pe.wait_ge(hid_lo_ready, steps + (FF_STEPS + j + 1))
                    for f in range(4):
                        q = unit((moe_first_unit(j + 1) + 8 if j < E_STEPS - 1 else E_UNITS - 4) + f)
                        for half in range(2):
                            cols = slice(half * 512, (half + 1) * 512)
                            m = three(ps[:, 3 + half, :], hid_hi[:, f * P:(f + 1) * P], hid_lo[:, f * P:(f + 1) * P],
                                      w_hi[:, q, cols], w_lo[:, q, cols], j == 0 and f == 0, j == E_STEPS - 1 and f == 3)
                        m.then_inc(unit_used, 1)

                pe.wait_ge(xg_lo_ready, i + 1)
                for j in range(E_STEPS):
                    if j == 1:
                        pe.wait_ge(acc_ready, i * 4 + 1)
                    else:
                        pe.wait_ge(silu_done, steps + (FF_STEPS + max(j - 1, 0)))
                    rows(j, 0, GATE_BANKS[j % 2])
                    if j == 1:
                        for t in range(TT):
                            m = pe.transpose(ps[:, 5, t * P:(t + 1) * P], sel[:, t, :], ident[:, :])
                        m.then_inc(selt_mm, 1)
                    if j >= 1:
                        turn(j - 1)
                    rows(j, 1, 1)
                    if j >= 1:
                        down(j - 1)
                turn(E_STEPS - 1)
                pe.wait_ge(selt_ready, i + 1)
                gather(i + 1)
                down(E_STEPS - 1)
                pe.wait_ge(xg_ready, i + 2)
                pe.wait_ge(xg2_ready, i + 2)
                for half in range(2):
                    pe.wait_ge(y_ready, i * 2 + (half + 1))
                    for t in range(TT):
                        pe.matmul(ps[:, SCATTER_BANKS[t][half], :], sel_t[:, t, :], y_hi[half],
                                  start=True, stop=False, skip_group_check=True)
                for half in range(2):
                    pe.wait_ge(y_lo_ready, i * 2 + (half + 1))
                    for t in range(TT):
                        pe.matmul(ps[:, SCATTER_BANKS[t][half], :], sel_t[:, t, :], y_lo[half][:, :],
                                  start=False, stop=True, skip_group_check=True).then_inc(scatter_mm, 1)

            with pe.Fori(0, E) as i:
                item(i)
            n_items = pe.value_load(plan_i[0:1, 0:1], min_val=E, max_val=ITEMS)
            for r in range(OVER):
                with pe.If(n_items > E + r):
                    item(E + r)


_INS = ['x', 'c', 'positions', 'w_in', 'q_norm_g', 'kv_norm_g', 'w_uq', 'w_ukv', 'conv_w', 'mix_norm_g', 'w_o',
        'w_ada', 'b_ada', 'ln1_g', 'ln1_b', 'ln2_g', 'ln2_b', 'ffn_w_gate', 'ffn_w_up', 'ffn_w_down',
        'moe_router_w', 'moe_router_b', 'moe_w_gate', 'moe_w_up', 'moe_w_down']


def kernel(**inputs):
    import numpy as _np
    import concourse.bacc as _bacc
    from concourse import mybir as _mybir
    from concourse.bass_utils import run_bass_kernel_spmd as _run

    nc = _bacc.Bacc("TRN2", target_bir_lowering=False, num_devices=1, dynamic_dma_scratch_size=1024)
    arrays, args = {}, {}
    for name in _INS:
        v = _np.ascontiguousarray(inputs[name])
        arrays[f"in_{name}_dram"] = v
        args[name] = nc.dram_tensor(f"in_{name}_dram", v.shape, _mybir.dt.from_np(v.dtype), kind="ExternalInput").ap()
    out = nc.dram_tensor("out_0_dram", (1, T, D), _mybir.dt.float32, kind="ExternalOutput").ap()
    trunk(nc, args, out)
    r = _run(nc, [arrays], core_ids=[0])
    return r.results[0]["out_0_dram"]
```
